# Optimizing a Trainium2 kernel written in Bass

```python
import math
import jax, jax.numpy as jnp
from jax import lax
import numpy as np

D_MODEL = 2048
BATCH = 1
SEQ = 256
DEPTH = 1

N_Q_HEADS = 16
N_KV_HEADS = 4
HEAD_DIM = 64
WINDOW = 128
ATTN_BLOCK = 128
N_BUCKETS = 32
MAX_DISTANCE = 128
GLA_HEADS = 4
GLA_DK = D_MODEL // 2 // GLA_HEADS
GLA_DV = D_MODEL // GLA_HEADS
GLA_LOWRANK = 16
GLA_NORMALIZER = 16.0
GLA_CHUNK = 64
D_FF = 5632
CONV_WIDTH = 3
EPS = 1e-6
NEG_INF = -1e30

ATTN_Q_W = N_Q_HEADS * HEAD_DIM
ATTN_KV_W = N_KV_HEADS * HEAD_DIM
GLA_K_W = GLA_HEADS * GLA_DK
GLA_V_W = GLA_HEADS * GLA_DV
IN_SPLITS = (ATTN_Q_W, ATTN_KV_W, ATTN_KV_W, GLA_K_W, GLA_K_W, GLA_V_W, GLA_V_W, GLA_LOWRANK, D_MODEL, D_MODEL)
D_IN = sum(IN_SPLITS)

kernel_name = "hybrid_swa_sink_gla_convffn_adaln"

def rms_norm(x, gain):
    xf = x.astype(jnp.float32)
    y = xf * lax.rsqrt(jnp.mean(xf * xf, axis=-1, keepdims=True) + EPS)
    return (y * gain.astype(jnp.float32)).astype(x.dtype)

def modulate(h, shift, scale):
    return h * (1 + scale[:, None, :]) + shift[:, None, :]

def t5_bucket(dist):
    max_exact = N_BUCKETS // 2
    d = jnp.maximum(dist, 0)
    large = max_exact + (jnp.log(jnp.maximum(d, 1).astype(jnp.float32) / max_exact)
                         / math.log(MAX_DISTANCE / max_exact) * (N_BUCKETS - max_exact)).astype(jnp.int32)
    large = jnp.minimum(large, N_BUCKETS - 1)
    return jnp.where(d < max_exact, d, large)

def sliding_window_attention(q, k, v, q_gain, k_gain, sinks, rel_bias_table):
    B, S = q.shape[0], q.shape[1]
    nb = S // ATTN_BLOCK
    G = N_Q_HEADS // N_KV_HEADS
    f32 = jnp.float32
    q = rms_norm(q, q_gain)
    k = rms_norm(k, k_gain)
    qb = q.reshape(B, nb, ATTN_BLOCK, N_KV_HEADS, G, HEAD_DIM)

    def band(t):
        tb = t.reshape(B, nb, ATTN_BLOCK, N_KV_HEADS, HEAD_DIM)
        prev = jnp.pad(tb, ((0, 0), (1, 0), (0, 0), (0, 0), (0, 0)))[:, :-1]
        return jnp.concatenate([prev, tb], axis=2)

    kb, vb = band(k), band(v)
    scores = jnp.einsum('bnqhgd,bnkhd->bhgnqk', qb, kb, preferred_element_type=f32) * (HEAD_DIM ** -0.5)

    i = jnp.arange(ATTN_BLOCK)[:, None]
    j = jnp.arange(2 * ATTN_BLOCK)[None, :]
    dist = i + ATTN_BLOCK - j
    in_window = (dist >= 0) & (dist < WINDOW)
    first_block = (jnp.arange(nb) == 0)[:, None, None]
    valid = in_window[None] & ~(first_block & (j < ATTN_BLOCK)[None])

    bias = rel_bias_table[t5_bucket(dist)].astype(f32)
    bias = bias.transpose(2, 0, 1).reshape(N_KV_HEADS, G, 1, ATTN_BLOCK, 2 * ATTN_BLOCK)
    scores = jnp.where(valid, scores + bias, NEG_INF)

    sink = sinks.astype(f32).reshape(N_KV_HEADS, G, 1, 1, 1)
    m = jnp.maximum(jnp.max(scores, axis=-1, keepdims=True), sink)
    p = jnp.exp(scores - m)
    probs = p / (jnp.sum(p, axis=-1, keepdims=True) + jnp.exp(sink - m))
    out = jnp.einsum('bhgnqk,bnkhd->bnqhgd', probs.astype(vb.dtype), vb)
    return out.reshape(B, S, ATTN_Q_W).astype(q.dtype)

def gated_linear_attention(q, k, v, gk_log, out_gate, o_gain):
    B, S = q.shape[0], q.shape[1]
    nc = S // GLA_CHUNK
    C = GLA_CHUNK
    f32 = jnp.float32

    def chunk(t):
        return t.astype(f32).reshape(B, nc, C, GLA_HEADS, t.shape[-1]).transpose(0, 3, 1, 2, 4)

    qc = chunk(q) * (GLA_DK ** -0.5)
    kc = chunk(k)
    vc = chunk(v)
    g = jnp.cumsum(chunk(gk_log), axis=3)
    g_last = g[:, :, :, -1:, :]
    q_dec = qc * jnp.exp(g)
    k_inv = kc * jnp.exp(-g)
    k_to_end = kc * jnp.exp(g_last - g)

    causal = jnp.tril(jnp.ones((C, C), dtype=bool))
    A = jnp.where(causal, jnp.einsum('bhnid,bhnjd->bhnij', q_dec, k_inv), 0.0)
    o_intra = jnp.einsum('bhnij,bhnjv->bhniv', A, vc)

    def step(state, inp):
        qd, kte, vv, decay = inp
        o = jnp.einsum('bhcd,bhdv->bhcv', qd, state)
        state = decay[..., None] * state + jnp.einsum('bhcd,bhcv->bhdv', kte, vv)
        return state, o

    xs = (jnp.moveaxis(q_dec, 2, 0), jnp.moveaxis(k_to_end, 2, 0), jnp.moveaxis(vc, 2, 0),
          jnp.moveaxis(jnp.exp(g_last[:, :, :, 0, :]), 2, 0))
    state0 = jnp.zeros((B, GLA_HEADS, GLA_DK, GLA_DV), f32)
    _, o_inter = lax.scan(step, state0, xs)
    o = o_intra + jnp.moveaxis(o_inter, 0, 2)
    o = o.transpose(0, 2, 3, 1, 4).reshape(B, S, GLA_HEADS, GLA_DV)
    o = rms_norm(o, o_gain) * jax.nn.silu(out_gate.astype(f32))
    return o.reshape(B, S, GLA_V_W).astype(q.dtype)

def conv_ffn(h, w_up, conv_w, conv_b, w_down):
    S = h.shape[1]
    u = h @ w_up
    up = jnp.pad(u, ((0, 0), (CONV_WIDTH - 1, 0), (0, 0)))
    y = conv_b
    for tap in range(CONV_WIDTH):
        y = y + conv_w[tap] * up[:, tap:tap + S]
    a, b = jnp.split(y, 2, axis=-1)
    return (jax.nn.silu(a) * b) @ w_down

def setup_inputs(seed: int = 0) -> dict:
    key = jax.random.key(seed)
    ks = jax.random.split(key, 24)
    f32 = jnp.float32
    L, D = DEPTH, D_MODEL

    def nrm(k, shape, scale):
        return jax.random.normal(k, shape, f32) * scale

    return {
        "x": nrm(ks[0], (BATCH, SEQ, D), 1.0),
        "c": nrm(ks[1], (BATCH, D), 1.0),
        "rel_bias_table": nrm(ks[2], (N_BUCKETS, N_Q_HEADS), 0.5),
        "w_ada": nrm(ks[3], (L, D, 6 * D), D ** -0.5),
        "b_ada": nrm(ks[4], (L, 6 * D), 0.02),
        "norm1_gain": 1.0 + nrm(ks[5], (L, D), 0.02),
        "w_in": nrm(ks[6], (L, D, D_IN), D ** -0.5),
        "q_norm_gain": 1.0 + nrm(ks[7], (L, HEAD_DIM), 0.02),
        "k_norm_gain": 1.0 + nrm(ks[8], (L, HEAD_DIM), 0.02),
        "attn_sinks": nrm(ks[9], (L, N_Q_HEADS), 0.5),
        "w_gk_up": nrm(ks[10], (L, GLA_LOWRANK, GLA_K_W), GLA_LOWRANK ** -0.5),
        "b_gk": nrm(ks[11], (L, GLA_K_W), 0.02),
        "gla_norm_gain": 1.0 + nrm(ks[12], (L, GLA_DV), 0.02),
        "w_branch_attn": nrm(ks[13], (L, ATTN_Q_W, D), ATTN_Q_W ** -0.5),
        "w_branch_gla": nrm(ks[14], (L, GLA_V_W, D), GLA_V_W ** -0.5),
        "w_out": nrm(ks[15], (L, D, D), D ** -0.5),
        "norm2_gain": 1.0 + nrm(ks[16], (L, D), 0.02),
        "w_ffn_up": nrm(ks[17], (L, D, 2 * D_FF), D ** -0.5),
        "ffn_conv_w": nrm(ks[18], (L, CONV_WIDTH, 2 * D_FF), CONV_WIDTH ** -0.5),
        "ffn_conv_b": nrm(ks[19], (L, 2 * D_FF), 0.02),
        "w_ffn_down": nrm(ks[20], (L, D_FF, D), D_FF ** -0.5),
    }

def reference(x, c, rel_bias_table, w_ada, b_ada, norm1_gain, w_in, q_norm_gain, k_norm_gain,
              attn_sinks, w_gk_up, b_gk, gla_norm_gain, w_branch_attn, w_branch_gla, w_out,
              norm2_gain, w_ffn_up, ffn_conv_w, ffn_conv_b, w_ffn_down):
    B, S = x.shape[0], x.shape[1]
    offsets = []
    acc = 0
    for width in IN_SPLITS[:-1]:
        acc += width
        offsets.append(acc)
    c_act = jax.nn.silu(c)

    for l in range(DEPTH):
        mod = c_act @ w_ada[l] + b_ada[l]
        shift1, scale1, gate1, shift2, scale2, gate2 = jnp.split(mod, 6, axis=-1)

        h = modulate(rms_norm(x, norm1_gain[l]), shift1, scale1)
        proj = h @ w_in[l]
        aq, ak, av, gq, gk, gv, gr, glr, ga, gb = jnp.split(proj, offsets, axis=-1)

        y_attn = sliding_window_attention(
            aq.reshape(B, S, N_Q_HEADS, HEAD_DIM),
            ak.reshape(B, S, N_KV_HEADS, HEAD_DIM),
            av.reshape(B, S, N_KV_HEADS, HEAD_DIM),
            q_norm_gain[l], k_norm_gain[l], attn_sinks[l], rel_bias_table)

        gk_log = jax.nn.log_sigmoid((glr @ w_gk_up[l] + b_gk[l]).astype(jnp.float32)) / GLA_NORMALIZER
        y_gla = gated_linear_attention(
            gq.reshape(B, S, GLA_HEADS, GLA_DK),
            gk.reshape(B, S, GLA_HEADS, GLA_DK),
            gv.reshape(B, S, GLA_HEADS, GLA_DV),
            gk_log.reshape(B, S, GLA_HEADS, GLA_DK),
            gr.reshape(B, S, GLA_HEADS, GLA_DV),
            gla_norm_gain[l])

        merged = (jax.nn.sigmoid(ga) * (y_attn @ w_branch_attn[l])
                  + jax.nn.sigmoid(gb) * (y_gla @ w_branch_gla[l]))
        x = x + gate1[:, None, :] * (merged @ w_out[l])

        h2 = modulate(rms_norm(x, norm2_gain[l]), shift2, scale2)
        x = x + gate2[:, None, :] * conv_ffn(h2, w_ffn_up[l], ffn_conv_w[l], ffn_conv_b[l], w_ffn_down[l])
    return x


_drawn_inputs = setup_inputs


def setup_inputs(seed=0):
    import zlib

    import numpy as np

    out = dict(_drawn_inputs(seed))
    spreads = {}
    factors = {'norm1_gain': 5.208,
     'q_norm_gain': 8.0,
     'k_norm_gain': 8.0,
     'attn_sinks': 200.0,
     'b_gk': 8.0,
     'gla_norm_gain': 8.0,
     'norm2_gain': 14.109,
     'ffn_conv_b': 16.573,
     'rel_bias_table': 5.2}
    for name, (base, spread) in spreads.items():
        noise = np.random.default_rng([zlib.crc32(name.encode()), seed]).standard_normal(out[name].shape)
        drawn = base * np.exp(spread * noise) if base else spread * noise
        out[name] = __import__('jax').numpy.asarray(drawn.astype(out[name].dtype))
    for name, factor in factors.items():
        out[name] = (out[name] * factor).astype(out[name].dtype)
    return out
```

```python
from contextlib import ExitStack

import numpy as np

import concourse.bass as bass
from concourse import mybir

F32 = mybir.dt.float32
F32R = mybir.dt.float32r
ALU = mybir.AluOpType
ACT = mybir.ActivationFunctionType
AX = mybir.AxisListType
ds = bass.ds

P = 128
D = 2048
T = 256
KT = D // P
NB = 512
NT = NB // P
HQ, HKV, DH = 16, 4, 64
NBUCKETS, MAXDIST = 32, 128
GH, DK, DV, LR, CH = 4, 256, 512, 16, 64
FF = 5632
FT = FF // P
D_IN = 11792
EPS = 1e-6
NEG = -1e30
MASKED = NEG

C_AQ, C_AKV, C_GQ, C_GV, C_GR, C_GLR = 0, 1024, 1536, 3584, 5632, 7680
C_GA, C_GB = 7696, 9744

SLOTS = 4
AHEAD = 4
ADA_SLOTS = 4
ADA_W = 1024
ADA_COLS = ADA_W // P

U_AKV = 0
U_AQ = 8
U_GQK = 24
U_GV = 56
U_GR = 88
U_MERGE = 120
MERGE_UNITS = 8 + 8 + 4 + 8
U_WOUT = U_MERGE + 4 * MERGE_UNITS
U_UP = U_WOUT + 32
UP_STEPS = FF // NB
U_DOWN = U_UP + 16 * UP_STEPS
DOWN_UNITS = FT // 2
UNITS = U_DOWN + 4 * DOWN_UNITS


def one_hot_distances():
    dist = (np.arange(2 * P - 1) - (P - 1)) % P
    half = NBUCKETS // 2
    large = half + (np.log(np.maximum(dist, 1) / half) / np.log(MAXDIST / half) * (NBUCKETS - half)).astype(np.int64)
    bucket = np.where(dist < half, dist, np.minimum(large, NBUCKETS - 1))
    return (np.arange(NBUCKETS)[:, None] == bucket[None, :]).astype(np.float32)


class Run:

    def __init__(self, base, i=None, per=0):
        self.base, self.i, self.per = base, i, per

    def at(self, k=0):
        return self.base + k if self.i is None else self.i * self.per + (self.base + k)

    def slot(self, k):
        return (self.base + k) % SLOTS

    def landed(self, k):
        n = 16 * ((self.base + k) // SLOTS + 1)
        return n if self.i is None else self.i * (16 * self.per // SLOTS) + n

    def shifted(self, k):
        return Run(self.base + k, self.i, self.per)


class Own:

    def __init__(self, eng, sem):
        self.eng, self.sem, self.n, self.i, self.per = eng, sem, 0, None, 0

    def __call__(self, instruction):
        instruction.then_inc(self.sem, 1)
        self.n += 1
        self.eng.wait_ge(self.sem, self.n if self.i is None else self.i * self.per + self.n)

    def enter(self, i, per):
        self.i, self.per, self.start = i, per, self.n

    def leave(self, turns):
        assert self.n - self.start == self.per, (self.n - self.start, self.per)
        self.n, self.i = self.start + turns * self.per, None


def layer(nc, x, c, rel, w_ada, b_ada, g1, w_in, qg, kg, sinks, wgk, bgk, ggla, wba, wbg, wo, g2,
          w_up, conv_w, conv_b, w_dn, onehot, out):
    xs = nc.dram_tensor("x_featuremajor", (P, KT, T), F32, kind="Internal").ap()
    w_in_u = w_in[0].rearrange("(u k p) n -> u p k n", k=2, p=P)
    wba_u = wba[0].rearrange("(u k p) n -> u p k n", k=2, p=P)
    wbg_u = wbg[0].rearrange("(u k p) n -> u p k n", k=2, p=P)
    wo_u = wo[0].rearrange("(u k p) n -> u p k n", k=2, p=P)
    up_u = w_up[0].rearrange("(u k p) n -> u p k n", k=2, p=P)
    dn_u = w_dn[0].rearrange("(u k p) n -> u p k n", k=2, p=P)
    ada_k = w_ada[0].rearrange("(k p) n -> p k n", p=P)
    out_t = out[0].rearrange("(t p) n -> p t n", p=P)

    KB = 1024
    base = 16512

    def sb(name, at, shape, dt=F32):
        return nc.alloc_sbuf_tensor_at(name, shape, dt, offset=base + int(at * KB))

    h_hi = sb("h_hi", 0, [P, KT, T], F32R)
    h_lo = sb("h_lo", 16, [P, KT, T], F32R)
    x1 = sb("x1", 0, [P, KT, T])
    h2_hi = sb("h2_hi", 16, [P, KT, T], F32R)
    h2_lo = sb("h2_lo", 32, [P, KT, T], F32R)
    xT = sb("xT", 32, [P, KT, T])
    gv = sb("gv", 32, [P, GH, 2, DV])
    yg_lo = sb("yg_lo", 32, [P, KT, T], F32R)
    bias = sb("bias", 48, [P, HQ, 2 * P])
    yg_hi = sb("yg_hi", 48, [P, KT, T], F32R)
    x_sq = sb("x_sq", 64, [P, KT, T])
    ya_hi = sb("ya_hi", 64, [P, 8, T], F32R)
    ya_lo = sb("ya_lo", 72, [P, 8, T], F32R)
    x_tok = sb("x_tok", 80, [P, 2, D])
    gqk = sb("gqk", 80, [P, 2 * 8, T])
    m_hi = sb("m_hi", 80, [P, KT, T], F32R)
    vrows = sb("vrows", 96, [P, 5, P])
    lg = sb("lg", 96, [P, 8, T])
    sig_a = sb("sig_a", 96, [P, NT, T])
    sig_b = sb("sig_b", 100, [P, NT, T])
    qT = sb("qT", 104, [P, 8, T])
    hot = sb("hot", 104, [NBUCKETS, 2 * P - 1])
    relt = sb("relt", 105, [NBUCKETS, HQ])
    kT = sb("kT", 112, [P, 2, T])
    kS = sb("kS", 114, [P, 2, T])
    vt = sb("vt", 116, [P, 2, 2 * P])
    sq = sb("sq", 118, [P, NT, T])
    rstd = sb("rstd", 122, [P, NT, T])
    p1 = sb("p1", 118, [P, NT, 2 * P])
    p0 = sb("p0", 122, [P, NT, P])
    pt = sb("pt", 124, [P, 3, NB])
    wgl = sb("wgl", 126, [P, KT, LR])
    wgl_hi = sb("wgl_hi", 127, [P, KT, LR], F32R)
    wgl_lo = sb("wgl_lo", 128, [P, KT, LR], F32R)
    glr = sb("glr", 129, [P, 2, LR])
    glrT = sb("glrT", 129.25, [LR, T])
    lnp = sb("lnp", 130, [P, 2, T])
    wgk_s = sb("wgk_s", 132, [LR, 8 * P])
    m_lo = sb("m_lo", 104, [P, KT, T], F32R)
    eg = sb("eg", 104, [P, 2, T])
    en = sb("en", 106, [P, 2, T])
    kx = sb("kx", 108, [P, 2, 3 * CH])
    qx = sb("qx", 109.5, [P, 2, 3 * CH])
    qd = sb("qd", 111, [P, 2, T])
    ki = sb("ki", 113, [P, 2, T])
    gvh = sb("gvh", 117, [P, 2, DV])
    osq = sb("osq", 121, [P, NT, T])
    sil = sb("sil", 125, [P, NT, T])
    yt = sb("yt", 129, [P, NT, T])
    rsg = sb("rsg", 133, [P, T])
    mrg = sb("mrg", 120, [P, NT, T])
    mrg2 = sb("mrg2", 124, [P, NT, T])
    xsq2 = sb("xsq2", 120, [P, NT, T])
    sqsum = sb("sqsum", 124, [P, T])
    sqpart = sb("sqpart", 125, [P, T])
    rs2 = sb("rs2", 126, [P, T])
    xr = sb("xr", 128, [P, NT, T])
    g_hi = sb("g_hi", 48, [P, FT, T], F32R)
    g_lo = sb("g_lo", 92, [P, FT, T], F32R)
    stage = sb("stage", 136, [P, SLOTS, 2, NB])
    w_hi = sb("w_hi", 152, [P, SLOTS, 2, NB], F32R)
    w_lo = sb("w_lo", 168, [P, SLOTS, 2, NB], F32R)
    ada = sb("ada", 184, [P, ADA_SLOTS, ADA_W])
    acc = sb("acc", 200, [P, ADA_W])
    cva = sb("cva", 184, [P, NT, T])
    cvb = sb("cvb", 188, [P, NT, T])
    ytmp = sb("ytmp", 184, [P, 2, NT, T])
    outs = sb("outs", 192, [P, 2, 2, NB])
    ident = sb("ident", 204, [P, P])
    ones = sb("ones", 204.5, [P, P])
    vec = sb("vec", 205, [P, 5, P])

    def small(name, row, col, shape):
        return sb(name, 205 + (row * P + col) * 4 / KB, shape)

    a1, a2 = small("a1", 2, 88, [P, KT]), small("a2", 2, 104, [P, KT])
    cact, snk = small("cact", 3, 88, [P, KT]), small("snk", 3, 104, [P, HQ])
    mx, nmx = small("mx", 4, 88, [P, 2, NT]), small("nmx", 4, 96, [P, 2, NT])
    esk, rsum = small("esk", 4, 104, [P, 2, NT]), small("rsum", 4, 112, [P, 2, NT])
    eps = small("eps", 1, 120, [P, 8])
    mod = small("mod", 4, 120, [P, 96])
    snkrow = sb("snkrow", 131.25, [1, HQ])
    halves = sb("halves", 130.5, [P, P])
    keep = sb("keep", 133, [P, T])
    at = sb("at", 115, [P, 384])

    ps = nc.alloc_psum_tensor("ps", [P, 2, NT, T], F32)
    b4 = nc.alloc_psum_tensor("b4", [P, NB], F32)
    b56 = nc.alloc_psum_tensor("b56", [P, NT, T], F32)
    b7 = nc.alloc_psum_tensor("b7", [P, NB], F32)
    ps_tok = ps[:].rearrange("p b j t -> p b (j t)").rearrange("p b (a n) -> p b a n", a=2)
    modp = b4[:, 0:ADA_COLS]
    hi_b4 = b4[:, T:2 * T]

    V_BADA = vec[:, 0, 0:96]
    V_G1 = vec[:, 0, 96:112]
    V_C = vec[:, 0, 112:128]
    V_G2 = vec[:, 1, 88:104]
    V_BGK = vec[:, 1, 104:112]
    V_GG = vec[:, 1, 112:116]
    V_QG = vec[:, 1, 116:117]
    V_KG = vec[:, 1, 117:118]

    with ExitStack() as ctx:
        def sem(name):
            return ctx.enter_context(nc.semaphore(name))

        stage_full = [sem(f"stage_full{i}") for i in range(SLOTS)]
        ada_full = [sem(f"ada_full{i}") for i in range(ADA_SLOTS)]
        hi_done = sem("hi_done")
        lo_done = sem("lo_done")
        used = sem("used")
        ps_free = [sem("ps_free0"), sem("ps_free1")]
        ada_done = sem("ada_done")
        mod_red = sem("mod_red")
        mod_ready = sem("mod_ready")
        acc_clear = sem("acc_clear")
        vec_in, x_in, misc_in = sem("vec_in"), sem("x_in"), sem("misc_in")
        consts, keep_ready = sem("consts"), sem("keep_ready")
        vec_tr, vec_ready = sem("vec_tr"), sem("vec_ready")
        x_tr, xT_act, xT_dve, xs_out = sem("x_tr"), sem("xT_act"), sem("xT_dve"), sem("xs_out")
        xsq_done, n1_sum, n1_rstd = sem("xsq_done"), sem("n1_sum"), sem("n1_rstd")
        cact_ready = sem("cact_ready")
        bias_ps, bias_sb, bias_ready = sem("bias_ps"), sem("bias_sb"), sem("bias_ready")
        snk_ps, snk_ready = sem("snk_ps"), sem("snk_ready")
        wgl_hi_done, wgl_ready = sem("wgl_hi_done"), sem("wgl_ready")
        hf_done, hhi_done, h_ready = sem("hf_done"), sem("hhi_done"), sem("h_ready")
        qk_sq, qk_sum, qk_rstd, k_ready, k_swapped = (
            sem("qk_sq"), sem("qk_sum"), sem("qk_rstd"), sem("k_ready"), sem("k_swapped"))
        scored, m_ready, exped, p_ready = sem("scored"), sem("m_ready"), sem("exped"), sem("p_ready")
        p_tr, pt_ready, pv_done, yahi_done, ya_ready = (
            sem("p_tr"), sem("pt_ready"), sem("pv_done"), sem("yahi_done"), sem("ya_ready"))
        glr_ps, glr_sb, glrT_ps, glrT_sb, z_ps, z_sb = (
            sem("glr_ps"), sem("glr_sb"), sem("glrT_ps"), sem("glrT_sb"), sem("z_ps"), sem("z_sb"))
        lnp_ready, lg_ready = sem("lnp_ready"), sem("lg_ready")
        gla_arg, gla_exp, gla_ready = sem("gla_arg"), sem("gla_exp"), sem("gla_ready")
        at_ps, at_sb, at_ready, gvh_ready = sem("at_ps"), sem("at_sb"), sem("at_ready"), sem("gvh_ready")
        at_zero = sem("at_zero")
        o_ps, osq_done, oss_ps, rsg_ready = sem("o_ps"), sem("osq_done"), sem("oss_ps"), sem("rsg_ready")
        sil_ln, sil_arg, sil_sig, yt_ready, yghi_done, yg_ready = (
            sem("sil_ln"), sem("sil_arg"), sem("sil_sig"), sem("yt_ready"), sem("yghi_done"), sem("yg_ready"))
        mrg_ready, mhi_done, m_done = sem("mrg_ready"), sem("mhi_done"), sem("m_done")
        x_back, x1sq_done, x1sum = sem("x_back"), sem("x1sq_done"), sem("x1sum")
        n2_sum, n2_rstd, h2f, h2hi_done, h2_ready = (
            sem("n2_sum"), sem("n2_rstd"), sem("h2f"), sem("h2hi_done"), sem("h2_ready"))
        cv0, sil_done, gf_done, ghi_done, g_ready = (
            sem("cv0"), sem("sil_done"), sem("gf_done"), sem("ghi_done"), sem("g_ready"))
        y_tr, outs_ready, stored = sem("y_tr"), sem("outs_ready"), sem("stored")
        act_own, dve_own, pool_own = sem("act_own"), sem("dve_own"), sem("pool_own")

        block = ctx.enter_context(nc.Block())

        @block.sync
        def _(sp):
            def load(u, k, src):
                if u.base + k >= SLOTS:
                    sp.wait_ge(lo_done, u.at(k - SLOTS + 1))
                sp.dma_start(stage[:, u.slot(k)], src).then_inc(stage_full[u.slot(k)], 16)

            def load_ada(a, k, kt, col):
                if a.base + k >= ADA_SLOTS:
                    sp.wait_ge(ada_done, a.at(k - ADA_SLOTS + 1))
                src = ada_k[:, kt, col] if isinstance(kt, int) else ada_k[:, ds(kt, 1), col].rearrange("p k n -> p (k n)")
                sp.dma_start(ada[:, a.slot(k)], src).then_inc(ada_full[a.slot(k)], 16)

            def store(b):
                sp.wait_ge(outs_ready, b + 1)
                sp.dma_start(out_t[:, :, b * NB:(b + 1) * NB], outs[:, b % 2]).then_inc(stored, 16)

            def rows(dram, n):
                return dram.rearrange("(r f) -> r f", f=n)

            sp.dma_start(vrows[0:96, 0, :], rows(b_ada[0], P)).then_inc(vec_in, 16)
            sp.dma_start(vrows[96:112, 0, :], rows(g1[0], P)).then_inc(vec_in, 16)
            sp.dma_start(vrows[112:128, 0, :], rows(c[0], P)).then_inc(vec_in, 16)
            sp.dma_start(x_tok[:], x[0].rearrange("(t p) n -> p t n", p=P)).then_inc(x_in, 16)
            sp.dma_start(vrows[0:88, 1, :], rows(conv_b[0], P)).then_inc(vec_in, 16)
            sp.dma_start(vrows[88:104, 1, :], rows(g2[0], P)).then_inc(vec_in, 16)
            sp.dma_start(vrows[104:112, 1, :], rows(bgk[0], P)).then_inc(vec_in, 16)
            sp.dma_start(vrows[112:116, 1, :], rows(ggla[0], P)).then_inc(vec_in, 16)
            for half in range(2):
                cols = slice(half * DH, (half + 1) * DH)
                sp.dma_start(vrows[116:117, 1, cols], qg).then_inc(vec_in, 16)
                sp.dma_start(vrows[117:118, 1, cols], kg).then_inc(vec_in, 16)
            for tap in range(3):
                sp.dma_start(vrows[0:88, 2 + tap, :], rows(conv_w[0, tap], P)).then_inc(vec_in, 16)
            sp.dma_start(relt[:], rel).then_inc(misc_in, 16)
            sp.dma_start(hot[:], onehot).then_inc(misc_in, 16)
            sp.dma_start(snkrow[:], sinks).then_inc(misc_in, 16)
            sp.dma_start(wgl[:], w_in[0, :, C_GLR:C_GLR + LR].rearrange("(k p) n -> p k n", p=P)).then_inc(misc_in, 16)
            sp.dma_start(wgk_s[:], wgk[0]).then_inc(misc_in, 16)

            u = Run(0)
            for k in range(4):
                load(u, k, w_in_u[k][:, :, C_AKV:C_AKV + NB])
            a = Run(0)
            for n in range(64):
                load_ada(a, n, n % KT, slice((n // KT) * ADA_W, (n // KT + 1) * ADA_W))
            for k in range(4, 8):
                load(u, k, w_in_u[k][:, :, C_AKV:C_AKV + NB])
            for b in range(2):
                for k in range(8):
                    load(Run(U_AQ + 8 * b), k, w_in_u[k][:, :, C_AQ + b * NB:C_AQ + (b + 1) * NB])
                if b == 0:
                    sp.wait_ge(k_ready, 1)
                    sp.dma_start(kS[0:DH], kT[DH:P]).then_inc(k_swapped, 16)
                    sp.dma_start(kS[DH:P], kT[0:DH]).then_inc(k_swapped, 16)

            def two_by_two(unit0, views, col0, chunk):
                with sp.Fori(0, 2) as i:
                    for b in range(2):
                        u = Run(unit0 + 8 * b, i, 16)
                        a = Run(KT * chunk + 4 * b, i, 8)
                        for k in range(8):
                            load(u, k, views[k][:, :, ds(i * (2 * NB) + (col0 + b * NB), NB)])
                            if k >= 4:
                                load_ada(a, k - 4, i * 8 + (4 * b + k - 4), slice(chunk * ADA_W, (chunk + 1) * ADA_W))

            two_by_two(U_GQK, w_in_u, C_GQ, 4)
            two_by_two(U_GV, w_in_u, C_GV, 5)
            two_by_two(U_GR, w_in_u, C_GR, 6)

            with sp.Fori(1, 5) as i:
                n0 = i * NB - NB
                a = Run(KT * 6, i, KT)
                kt = 0
                first = 0
                for src, units, col0, extra in ((w_in_u, 8, C_GA, (1, 1, 1, 2)), (w_in_u, 8, C_GB, (1, 1, 1, 2)),
                                                (wba_u, 4, 0, ()), (wbg_u, 8, 0, (1, 2, 1, 2))):
                    u = Run(U_MERGE - MERGE_UNITS + first, i, MERGE_UNITS)
                    for k in range(units):
                        load(u, k, src[k][:, :, ds(n0 + col0, NB)])
                        for _ in range(extra[k - 4] if k >= 4 and extra else 0):
                            load_ada(a, kt, kt, ds(i * ADA_W + 6 * ADA_W, ADA_W))
                            kt += 1
                    first += units

            sp.wait_ge(used, U_WOUT - 12)
            sp.dma_start(x1[:], xs).then_inc(x_back, 16)
            two_by_two(U_WOUT, wo_u, 0, 11)

            with sp.Fori(0, UP_STEPS) as i:
                for b in range(2):
                    u = Run(U_UP + 8 * b, i, 16)
                    for k in range(8):
                        load(u, k, up_u[k][:, :, ds(i * NB + b * FF, NB)])

            for b in range(4):
                for k in range(DOWN_UNITS):
                    load(Run(U_DOWN + b * DOWN_UNITS), k, dn_u[k][:, :, b * NB:(b + 1) * NB])
                    if b and k == 8:
                        store(b - 1)
            store(3)
            sp.wait_ge(stored, 16 * 4)

        @block.gpsimd
        def _(pool):
            own = Own(pool, pool_own)

            own(pool.memset(ident[:], 1.0))
            own(pool.affine_select(out=ident[:], in_=ident[:], compare_op=ALU.is_equal, fill=0.0, base=0,
                                   pattern=[[-1, P]], channel_multiplier=1))
            own(pool.memset(ones[:], 1.0))
            own(pool.memset(halves[:], 0.0))
            own(pool.memset(halves[0:DH, 0:DH], 1.0))
            own(pool.memset(halves[DH:P, DH:P], 1.0))
            pool.memset(eps[:], EPS).then_inc(consts, 1)
            pool.wait_ge(consts, 1)
            pool.wait_ge(bias_sb, 2)
            pool.affine_select(out=bias[:, :, P:2 * P], in_=bias[:, :, P:2 * P], compare_op=ALU.is_ge, fill=MASKED,
                               base=0, pattern=[[0, HQ], [-1, P]], channel_multiplier=1).then_inc(bias_ready, 1)
            pool.wait_ge(bias_ready, 1)
            pool.affine_select(out=bias[:, :, 0:P], in_=bias[:, :, 0:P], compare_op=ALU.is_gt, fill=MASKED,
                               base=0, pattern=[[0, HQ], [1, P]], channel_multiplier=-1).then_inc(bias_ready, 1)
            pool.wait_ge(bias_ready, 2)
            pool.wait_ge(z_sb, 8)
            own(pool.memset(keep[:], 1.0))
            pool.memset(keep[:].rearrange("p (c t) -> p c t", t=CH)[:, :, 0:1], 0.0).then_inc(keep_ready, 1)
            pool.wait_ge(keep_ready, 1)
            pool.wait_ge(pv_done, 4)
            pool.wait_ge(p_ready, 4)
            pool.wait_ge(ps_free[0], 6)
            pool.wait_ge(ps_free[1], 5)
            pool.memset(at[:], 0.0).then_inc(at_zero, 1)
            pool.wait_ge(at_zero, 1)
            for h in range(GH):
                if h:
                    pool.wait_ge(o_ps, h)
                    pool.wait_ge(at_ready, 2 * h)
                pool.tensor_copy(gvh[:].rearrange("p a n -> p (a n)"),
                                 gv[:, h].rearrange("p a n -> p (a n)")).then_inc(gvh_ready, 1)
                pool.wait_ge(gvh_ready, h + 1)
                pool.wait_ge(at_sb, h + 1)
                pool.affine_select(out=at[:, 0:T], in_=at[:, 0:T], compare_op=ALU.is_ge, fill=0.0, base=0,
                                   pattern=[[1, T]], channel_multiplier=-1).then_inc(at_ready, 1)
                pool.wait_ge(at_ready, 2 * h + 1)
                pool.affine_select(out=at[:, T:T + P], in_=at[:, T:T + P], compare_op=ALU.is_ge, fill=0.0, base=0,
                                   pattern=[[1, P]], channel_multiplier=-1).then_inc(at_ready, 1)

        @block.scalar
        def _(act):
            own = Own(act, act_own)

            def hi(u, k):
                act.wait_ge(stage_full[u.slot(k)], u.landed(k))
                if u.base + k >= SLOTS:
                    act.wait_ge(used, u.at(k - SLOTS + 1))
                act.activation(w_hi[:, u.slot(k)], stage[:, u.slot(k)], ACT.Copy).then_inc(hi_done, 1)

            def rstd_of(dst, src, n):
                own(act.activation(dst, src, ACT.Ln, scale=1.0 / n, bias=eps[:, 0:1]))
                return act.activation(dst, dst, ACT.Exp, scale=-0.5)

            def results_out(b):
                act.wait_ge(y_tr, b + 1)
                if b >= 2:
                    act.wait_ge(stored, 16 * (b - 1))
                act.activation(outs[:, b % 2], b56[:].rearrange("p (a j) t -> p a (j t)", a=2), ACT.Copy).then_inc(outs_ready, 1)

            act.wait_ge(vec_ready, 1)
            act.activation(cact[:], V_C, ACT.Silu).then_inc(cact_ready, 1)
            for b in range(2):
                act.wait_ge(x_tr, 4 * (b + 1))
                act.activation(xT[:, 4 * b:4 * b + 4], ps[:, b], ACT.Copy).then_inc(xT_act, 1)
            act.wait_ge(xT_act, 2)
            act.wait_ge(xT_dve, 3)
            act.dma_start(xs, xT[:]).then_inc(xs_out, 16)
            for b in range(4):
                act.activation(x_sq[:, 4 * b:4 * b + 4], xT[:, 4 * b:4 * b + 4], ACT.Square).then_inc(xsq_done, 1)
            u = Run(0)
            for k in range(4):
                hi(u, k)
            act.wait_ge(consts, 1)
            act.wait_ge(n1_sum, 1)
            rstd_of(rstd[:, 0], b7[:, 0:T], D).then_inc(n1_rstd, 1)
            act.wait_ge(misc_in, 16 * 5)
            act.activation(wgl_hi[:], wgl[:], ACT.Copy).then_inc(wgl_hi_done, 1)
            act.wait_ge(bias_ps, 1)
            by_head = ps[:].rearrange("p b j t -> p (b j t)").rearrange("p (j h) -> p h j", h=HQ)
            act.activation(bias[:, :, P:2 * P], by_head, ACT.Copy).then_inc(bias_sb, 1)
            act.activation(bias[:, :, 0:P], by_head, ACT.Copy).then_inc(bias_sb, 1)
            for g in range(4):
                act.wait_ge(hf_done, g + 1)
                act.activation(h_hi[:, 4 * g:4 * g + 4], xT[:, 4 * g:4 * g + 4], ACT.Copy).then_inc(hhi_done, 1)

            for b in range(3):
                u = Run(8 * b)
                for k in range(AHEAD, 8 + AHEAD):
                    hi(u, k)
                tiles = 2 if b == 0 else 4
                act.wait_ge(used, 8 * b + 8)
                if b:
                    act.wait_ge(ps_free[(b - 1) % 2], 1)
                act.activation(sq[:, 0:tiles], ps[:, b % 2, 0:tiles], ACT.Square).then_inc(qk_sq, 1)
                act.wait_ge(qk_sum, b + 1)
                rstd_of(rstd[:, 0:tiles], b56[:, 0:tiles], DH).then_inc(qk_rstd, 1)

            with act.Fori(0, 2) as i:
                for b in range(2):
                    u = Run(U_GQK + 8 * b, i, 16)
                    for k in range(AHEAD, 8 + AHEAD):
                        hi(u, k)

            for m in range(8):
                act.wait_ge(z_ps, m // 2 * 2 + 2)
                zp = b56[:, m] if m < 4 else b7[:, (m - 4) * T:(m - 3) * T] if m < 6 else b56[:, m - 6]
                act.activation(lg[:, m], zp, ACT.Identity, bias=V_BGK[:, m:m + 1]).then_inc(z_sb, 1)
            act.wait_ge(z_sb, 8)

            for g in range(4):
                u = Run(U_GV + 8 * g)
                hi(u, 4)
                if g:
                    act.wait_ge(lg_ready, g)
                own(act.activation(lnp[:], lg[:, 2 * g:2 * g + 2], ACT.Abs))
                own(act.activation(lnp[:], lnp[:], ACT.Exp, scale=-1.0))
                act.activation(lnp[:], lnp[:], ACT.Ln, bias=1.0).then_inc(lnp_ready, 1)
                for k in range(5, 8):
                    hi(u, k)
                act.wait_ge(m_ready, g + 1)
                for t in range(NT):
                    own(act.activation(p0[:, t], p0[:, t], ACT.Exp, bias=nmx[:, 0, t:t + 1], accum_out=rsum[:, 0, t:t + 1]))
                hi(u, 8)
                for t in range(NT):
                    own(act.activation(p1[:, t], p1[:, t], ACT.Exp, bias=nmx[:, 1, t:t + 1], accum_out=rsum[:, 1, t:t + 1]))
                act.activation(esk[:], esk[:], ACT.Exp).then_inc(exped, 1)
                for k in range(9, 12):
                    hi(u, k)
                act.wait_ge(p_tr, g + 1)
                own(act.activation(pt[:, 0], b7[:], ACT.Copy))
                act.activation(pt[:, 1:3], b56[:], ACT.Copy).then_inc(pt_ready, 1)
                act.wait_ge(pv_done, g + 1)
                act.activation(ya_hi[:, 2 * g:2 * g + 2].rearrange("p t (n q) -> p t n q", n=2),
                               b7[:].rearrange("p (n t q) -> p t n q", n=2, t=2), ACT.Copy).then_inc(yahi_done, 1)

            act.wait_ge(lg_ready, 4)
            act.wait_ge(p_ready, 4)
            with act.Fori(0, 2) as i:
                own.enter(i, 2 * 5)
                for k in range(2):
                    n = i * 2 + k
                    u = Run(U_GR + 8 * k, i, 16)
                    hi(u, 4)
                    act.activation(eg[:], lg[:, ds(i * 4 + 2 * k, 2)], ACT.Exp, scale=1 / 16).then_inc(gla_exp, 1)
                    act.activation(en[:], lg[:, ds(i * 4 + 2 * k, 2)], ACT.Exp, scale=-1 / 16).then_inc(gla_exp, 1)
                    hi(u, 5)
                    act.wait_ge(gla_arg, n + 1)
                    act.activation(kx[:], kx[:], ACT.Exp, scale=1 / 16).then_inc(gla_exp, 1)
                    act.activation(qx[:], qx[:], ACT.Exp, scale=1 / 16).then_inc(gla_exp, 1)
                    for q in range(6, 9):
                        hi(u, q)
                    act.wait_ge(at_zero, 1)
                    act.wait_ge(at_ps, n + 1)
                    own(act.activation(at[0:CH, 0:T], b7[0:CH, 0:T], ACT.Copy))
                    own(act.activation(at[CH:P, CH:T], b7[CH:P, CH:T], ACT.Copy))
                    own(act.activation(at[0:CH, T:T + P], b7[0:CH, T:T + P], ACT.Copy))
                    act.activation(at[CH:P, T + CH:T + P], b7[CH:P, T + CH:T + P], ACT.Copy).then_inc(at_sb, 1)
                    hi(u, 9)
                    act.wait_ge(o_ps, n + 1)
                    act.activation(osq[:], b56[:], ACT.Square).then_inc(osq_done, 1)
                    hi(u, 10)
                    act.wait_ge(oss_ps, n + 1)
                    rstd_of(rsg[:], hi_b4, DV).then_inc(rsg_ready, 1)
                    hi(u, 11)
                    act.wait_ge(used, u.at(8))
                    par = (1 + k) % 2
                    own(act.activation(sil[:], ps[:, par], ACT.Abs))
                    act.activation(sil[:], sil[:], ACT.Exp, scale=-1.0).then_inc(sil_ln, 1)
                    act.wait_ge(sil_ln, i * 4 + (2 * k + 1))
                    act.activation(sil[:], sil[:], ACT.Ln, bias=1.0).then_inc(sil_ln, 1)
                    act.wait_ge(sil_arg, n + 1)
                    act.activation(sil[:], sil[:], ACT.Exp).then_inc(sil_sig, 1)
                    act.wait_ge(yt_ready, n + 1)
                    act.activation(yg_hi[:, ds(i * 8 + 4 * k, 4)], yt[:], ACT.Copy).then_inc(yghi_done, 1)
                own.leave(2)

            with act.Fori(0, 4) as i:
                first = 0
                for b, (units, sig) in enumerate(((8, sig_a), (8, sig_b), (4, None), (8, None))):
                    u = Run(U_MERGE + first, i, MERGE_UNITS)
                    for k in range(AHEAD, units + AHEAD):
                        hi(u, k)
                    if sig is not None:
                        act.wait_ge(used, u.at(units))
                        act.activation(sig[:], ps[:, (1 + b) % 2], ACT.Sigmoid).then_inc(ps_free[(1 + b) % 2], 1)
                    first += units
                act.wait_ge(mrg_ready, i + 1)
                act.activation(m_hi[:, ds(i * 4, 4)], mrg[:], ACT.Copy).then_inc(mhi_done, 1)

            with act.Fori(0, 2) as i:
                for b in range(2):
                    u = Run(U_WOUT + 8 * b, i, 16)
                    for k in range(AHEAD, 8 + AHEAD):
                        hi(u, k)
                    act.wait_ge(ps_free[(1 + b) % 2], i + (16 + b))
                    act.activation(xsq2[:], x1[:, ds(i * 8 + 4 * b, 4)], ACT.Square).then_inc(x1sq_done, 1)
            act.wait_ge(n2_sum, 1)
            rstd_of(rs2[:], b7[:, 0:T], D).then_inc(n2_rstd, 1)
            for g in range(4):
                act.wait_ge(h2f, g + 1)
                act.activation(h2_hi[:, 4 * g:4 * g + 4], xr[:], ACT.Copy).then_inc(h2hi_done, 1)

            with act.Fori(0, UP_STEPS) as i:
                for b, cv in enumerate((cva, cvb)):
                    u = Run(U_UP + 8 * b, i, 16)
                    for k in range(AHEAD, 8 + AHEAD):
                        hi(u, k)
                    act.wait_ge(used, u.at(8))
                    for j in range(NT):
                        col = i * NT + (b * FT + j)
                        act.activation(cv[:, j], ps[:, (1 + b) % 2, j], ACT.Identity,
                                       scale=vec[:, 4, ds(col, 1)], bias=vec[:, 1, ds(col, 1)]).then_inc(cv0, 1)
                    if b == 0:
                        act.wait_ge(ps_free[1], i + 18)
                        act.activation(cva[:], cva[:], ACT.Silu).then_inc(sil_done, 1)
                act.wait_ge(gf_done, i + 1)
                act.activation(g_hi[:, ds(i * NT, NT)], cvb[:], ACT.Copy).then_inc(ghi_done, 1)

            for b in range(4):
                u = Run(U_DOWN + b * DOWN_UNITS)
                for k in range(AHEAD, DOWN_UNITS + AHEAD):
                    if u.base + k < UNITS:
                        hi(u, k)
                    if b and k == 8:
                        results_out(b - 1)
            results_out(3)

        @block.vector
        def _(dve):
            own = Own(dve, dve_own)
            TT, TS, STT = dve.tensor_tensor, dve.tensor_scalar, dve.scalar_tensor_tensor

            def lo(u, k):
                dve.wait_ge(hi_done, u.at(k + 1))
                TT(w_lo[:, u.slot(k)], stage[:, u.slot(k)], w_hi[:, u.slot(k)].bitcast(F32), ALU.subtract).then_inc(lo_done, 1)

            def times_c(a, k, kt):
                dve.wait_ge(ada_full[a.slot(k)], a.landed(k))
                if a.base + k:
                    dve.wait_ge(ada_done, a.at(k))
                cc = cact[:, kt:kt + 1] if isinstance(kt, int) else cact[:, ds(kt, 1)]
                STT(out=acc[:], in0=ada[:, a.slot(k)], scalar=cc, in1=acc[:], op0=ALU.mult, op1=ALU.add).then_inc(ada_done, 1)

            def clear_acc():
                own(dve.memset(acc[:], 0.0))

            def take_mod(chunk):
                dve.wait_ge(mod_red, chunk + 1)
                TT(mod[:, 8 * chunk:8 * chunk + 8], modp, V_BADA[:, 8 * chunk:8 * chunk + 8], ALU.add).then_inc(mod_ready, 1)
                clear_acc()

            def h_lo_of(g):
                dve.wait_ge(hhi_done, g + 1)
                TT(h_lo[:, 4 * g:4 * g + 4], xT[:, 4 * g:4 * g + 4], h_hi[:, 4 * g:4 * g + 4].bitcast(F32), ALU.subtract).then_inc(h_ready, 1)

            dve.wait_ge(vec_tr, 5)
            own(dve.tensor_copy(vec[:, 0], b56[:, 0, 0:P]))
            dve.tensor_copy(vec[:, 1, 0:118], b56[:, 0, P:P + 118]).then_inc(vec_ready, 1)
            own(dve.tensor_copy(vec[:, 2, 0:88], b56[:, 1, 0:88]))
            own(dve.tensor_copy(vec[:, 3, 0:88], b56[:, 1, P:P + 88]))
            dve.tensor_copy(vec[:, 4, 0:88], b56[:, 2, 0:88]).then_inc(vec_ready, 1)
            clear_acc()
            dve.wait_ge(x_tr, 16)
            dve.tensor_copy(xT[:, 8:10], b4[:].rearrange("p (a t) -> p a t", a=2)).then_inc(xT_dve, 1)
            dve.tensor_copy(xT[:, 10:14], b56[:]).then_inc(xT_dve, 1)
            dve.tensor_copy(xT[:, 14:16], b7[:].rearrange("p (a t) -> p a t", a=2)).then_inc(xT_dve, 1)
            dve.wait_ge(cact_ready, 1)
            a = Run(0)
            u = Run(0)
            for n in range(64):
                if n and n % KT == 0:
                    take_mod(n // KT - 1)
                times_c(a, n, n % KT)
                if n in (17, 18, 19, 20):
                    lo(u, n - 17)
                if n == 10:
                    dve.wait_ge(snk_ps, 1)
                    dve.tensor_copy(snk[:], b4[:, 16:32]).then_inc(snk_ready, 1)
                if n == 26:
                    dve.wait_ge(n1_rstd, 1)
                    dve.wait_ge(xs_out, 16)
                    dve.wait_ge(xsq_done, 4)
                    own(TT(xT[:, 0:8], xT[:, 0:8], rstd[:, 0:1].broadcast_to([P, 8, T]), ALU.mult))
                    own(TT(xT[:, 8:16], xT[:, 8:16], rstd[:, 0:1].broadcast_to([P, 8, T]), ALU.mult))
                if n == 40:
                    dve.wait_ge(wgl_hi_done, 1)
                    TT(wgl_lo[:], wgl[:], wgl_hi[:].bitcast(F32), ALU.subtract).then_inc(wgl_ready, 1)
            take_mod(3)
            dve.wait_ge(mod_ready, 4)
            own(STT(out=a1[:], in0=mod[:, KT:2 * KT], scalar=1.0, in1=V_G1, op0=ALU.add, op1=ALU.mult))
            for g in range(4):
                for j in range(4):
                    kt = 4 * g + j
                    f = TS(xT[:, kt], xT[:, kt], a1[:, kt:kt + 1], mod[:, kt:kt + 1], ALU.mult, ALU.add)
                    if j < 3:
                        own(f)
                    else:
                        f.then_inc(hf_done, 1)
                if g:
                    h_lo_of(g - 1)
            h_lo_of(3)

            for b in range(3):
                u = Run(8 * b)
                for k in range(AHEAD, 8 + AHEAD):
                    lo(u, k)
                dve.wait_ge(qk_rstd, b + 1)
                if b == 0:
                    STT(out=kT[:], in0=ps[:, 0, 0:2], scalar=V_KG, in1=rstd[:, 0:2], op0=ALU.mult, op1=ALU.mult).then_inc(k_ready, 1)
                    dve.tensor_copy(vt[:], ps[:, 0, 2:4]).then_inc(ps_free[0], 1)
                else:
                    dst = qT[:, 4 * (b - 1):4 * b]
                    STT(out=dst, in0=ps[:, b % 2], scalar=V_QG, in1=rstd[:], op0=ALU.mult, op1=ALU.mult).then_inc(ps_free[b % 2], 1)
            dve.wait_ge(glr_ps, 1)
            dve.tensor_copy(glr[:], b4[:, T:T + 2 * LR].rearrange("p (a n) -> p a n", a=2)).then_inc(glr_sb, 1)

            with dve.Fori(0, 2) as i:
                for b in range(2):
                    u = Run(U_GQK + 8 * b, i, 16)
                    a = Run(KT * 4 + 4 * b, i, 8)
                    for k in range(AHEAD, 8 + AHEAD):
                        lo(u, k)
                        if k < 8:
                            times_c(a, k - 4, i * 8 + (4 * b + k - 4))
                    dve.wait_ge(used, u.at(8))
                    TS(gqk[:, ds(i * 8 + 4 * b, 4)], ps[:, (1 + b) % 2], 1.0, None, ALU.mult).then_inc(ps_free[(1 + b) % 2], 1)
            dve.wait_ge(glrT_ps, 2)
            dve.tensor_copy(glrT[:], b4[0:LR, T:2 * T]).then_inc(glrT_sb, 1)
            take_mod(4)

            for g in range(4):
                u = Run(U_GV + 8 * g)
                a = Run(KT * 5 + 4 * g)
                par = (1 + g) % 2
                lo(u, 4)
                times_c(a, 0, 4 * g)
                dve.wait_ge(scored, g + 1)
                dve.wait_ge(bias_ready, 2)
                if g:
                    dve.wait_ge(p_tr, g)
                for half in range(2):
                    heads = bias[:, 4 * g + half:4 * g + 4:2, :]
                    even0 = (b7[:, 0:T] if half == 0 else hi_b4).rearrange("p (h k) -> p h k", h=2)
                    own(STT(out=p0[:, half:NT:2], in0=even0, scalar=DH ** -0.5, in1=heads[:, :, P:2 * P], op0=ALU.mult, op1=ALU.add))
                    own(STT(out=p1[:, half:NT:2], in0=b56[:, 2 * half:2 * half + 2], scalar=DH ** -0.5, in1=heads, op0=ALU.mult, op1=ALU.add))
                lo(u, 5)
                times_c(a, 1, 4 * g + 1)
                own(dve.tensor_reduce(mx[:, 0], p0[:], AX.X, ALU.max))
                own(dve.tensor_reduce(mx[:, 1], p1[:], AX.X, ALU.max))
                sink = snk[:, 4 * g:4 * g + 4].unsqueeze(1).broadcast_to([P, 2, NT])
                own(TT(mx[:], mx[:], sink, ALU.max))
                own(TS(nmx[:], mx[:], -1.0, None, ALU.mult))
                TT(esk[:], sink, mx[:], ALU.subtract).then_inc(m_ready, 1)
                lo(u, 6)
                times_c(a, 2, 4 * g + 2)
                dve.wait_ge(lnp_ready, g + 1)
                dve.wait_ge(keep_ready, 1)
                own(STT(out=lg[:, 2 * g:2 * g + 2], in0=lg[:, 2 * g:2 * g + 2], scalar=0.0, in1=lnp[:], op0=ALU.min, op1=ALU.subtract))
                own(dve.tensor_tensor_scan(lg[:, 2 * g], keep[:], lg[:, 2 * g], 0.0, ALU.mult, ALU.add))
                dve.tensor_tensor_scan(lg[:, 2 * g + 1], keep[:], lg[:, 2 * g + 1], 0.0, ALU.mult, ALU.add).then_inc(lg_ready, 1)
                lo(u, 7)
                times_c(a, 3, 4 * g + 3)
                lo(u, 8)
                dve.wait_ge(exped, g + 1)
                own(TT(rsum[:], rsum[:], esk[:], ALU.add))
                own(dve.reciprocal(rsum[:], rsum[:]))
                own(TT(p0[:], p0[:], rsum[:, 0].unsqueeze(2).broadcast_to([P, NT, P]), ALU.mult))
                TT(p1[:], p1[:], rsum[:, 1].unsqueeze(2).broadcast_to([P, NT, 2 * P]), ALU.mult).then_inc(p_ready, 1)
                for k in range(9, 12):
                    lo(u, k)
                dve.wait_ge(used, u.at(8))
                dve.tensor_copy(gv[:, g], ps_tok[:, par]).then_inc(ps_free[par], 1)
                dve.wait_ge(yahi_done, g + 1)
                TT(ya_lo[:, 2 * g:2 * g + 2].rearrange("p t (n q) -> p t n q", n=2),
                   b7[:].rearrange("p (n t q) -> p t n q", n=2, t=2),
                   ya_hi[:, 2 * g:2 * g + 2].rearrange("p t (n q) -> p t n q", n=2).bitcast(F32), ALU.subtract).then_inc(ya_ready, 1)
            take_mod(5)

            dve.wait_ge(lg_ready, 4)
            dve.wait_ge(pv_done, 4)
            with dve.Fori(0, 2) as i:
                own.enter(i, 2 * 10)
                for k in range(2):
                    n = i * 2 + k
                    par = (1 + k) % 2
                    u = Run(U_GR + 8 * k, i, 16)
                    a = Run(KT * 6 + 4 * k, i, 8)
                    lo(u, 4)
                    times_c(a, 0, i * 8 + 4 * k)
                    cum = lg[:, ds(i * 4 + 2 * k, 2)].rearrange("p t (c j) -> p t c j", j=CH)
                    last = cum[:, :, :, CH - 1:CH]
                    qv = gqk[:, ds(i * 4 + 2 * k, 2)]
                    kv = gqk[:, ds(i * 4 + (2 * k + 8), 2)]
                    own(TT(kx[:].rearrange("p t (c j) -> p t c j", j=CH), last[:, :, 0:3].broadcast_to([P, 2, 3, CH]),
                           cum[:, :, 0:3], ALU.subtract))
                    q3 = qx[:].rearrange("p t (c j) -> p t c j", j=CH)
                    own(TT(q3[:, :, 0:3:2], cum[:, :, 2:4], last[:, :, 1:3].broadcast_to([P, 2, 2, CH]), ALU.add))
                    TT(q3[:, :, 1:2], q3[:, :, 2:3], last[:, :, 1:2].broadcast_to([P, 2, 1, CH]), ALU.add).then_inc(gla_arg, 1)
                    lo(u, 5)
                    times_c(a, 1, i * 8 + (4 * k + 1))
                    dve.wait_ge(gla_exp, i * 8 + (4 * k + 4))
                    own(STT(out=qd[:], in0=qv, scalar=DK ** -0.5, in1=eg[:], op0=ALU.mult, op1=ALU.mult))
                    own(TT(ki[:], kv, en[:], ALU.mult))
                    own(TT(kx[:], kv[:, :, 0:3 * CH], kx[:], ALU.mult))
                    own(STT(out=qx[:, :, 0:2 * CH], in0=qv[:, :, 2 * CH:T], scalar=DK ** -0.5, in1=qx[:, :, 0:2 * CH], op0=ALU.mult, op1=ALU.mult))
                    STT(out=qx[:, :, 2 * CH:3 * CH], in0=qv[:, :, 3 * CH:T], scalar=DK ** -0.5, in1=qx[:, :, 2 * CH:3 * CH], op0=ALU.mult, op1=ALU.mult).then_inc(gla_ready, 1)
                    lo(u, 6)
                    times_c(a, 2, i * 8 + (4 * k + 2))
                    lo(u, 7)
                    times_c(a, 3, i * 8 + (4 * k + 3))
                    for q in range(8, 12):
                        lo(u, q)
                    dve.wait_ge(rsg_ready, n + 1)
                    for j in range(NT):
                        own(STT(out=yt[:, j], in0=b56[:, j], scalar=V_GG[:, j:j + 1], in1=rsg[:], op0=ALU.mult, op1=ALU.mult))
                    dve.wait_ge(sil_ln, i * 4 + (2 * k + 2))
                    STT(out=sil[:], in0=ps[:, par], scalar=0.0, in1=sil[:], op0=ALU.min, op1=ALU.subtract).then_inc(sil_arg, 1)
                    dve.wait_ge(sil_sig, n + 1)
                    TT(sil[:], ps[:, par], sil[:], ALU.mult).then_inc(ps_free[par], 1)
                    dve.wait_ge(ps_free[par], i + (6 + k))
                    TT(yt[:], yt[:], sil[:], ALU.mult).then_inc(yt_ready, 1)
                    dve.wait_ge(yghi_done, n + 1)
                    TT(yg_lo[:, ds(i * 8 + 4 * k, 4)], yt[:], yg_hi[:, ds(i * 8 + 4 * k, 4)].bitcast(F32), ALU.subtract).then_inc(yg_ready, 1)
                own.leave(2)
            take_mod(6)

            with dve.Fori(0, 4) as i:
                own.enter(i, 1)
                a = Run(KT * 7, i, KT)
                kt = 0
                first = 0
                for b, (units, extra) in enumerate(((8, (1, 1, 1, 2)), (8, (1, 1, 1, 2)), (4, ()), (8, (1, 2, 1, 2)))):
                    u = Run(U_MERGE + first, i, MERGE_UNITS)
                    par = (1 + b) % 2
                    for k in range(AHEAD, units + AHEAD):
                        lo(u, k)
                        for _ in range(extra[k - 4] if k < 8 and extra else 0):
                            times_c(a, kt, kt)
                            kt += 1
                    if b >= 2:
                        dve.wait_ge(used, u.at(units))
                        dve.wait_ge(ps_free[par], i * 2 + (6 + b))
                        if b == 2:
                            TT(mrg[:], ps[:, par], sig_a[:], ALU.mult).then_inc(ps_free[par], 1)
                        else:
                            TT(mrg2[:], ps[:, par], sig_b[:], ALU.mult).then_inc(ps_free[par], 1)
                            dve.wait_ge(ps_free[1], i * 2 + 9)
                            dve.wait_ge(ps_free[0], i * 2 + 10)
                            TT(mrg[:], mrg[:], mrg2[:], ALU.add).then_inc(mrg_ready, 1)
                            dve.wait_ge(mhi_done, i + 1)
                            TT(m_lo[:, ds(i * 4, 4)], mrg[:], m_hi[:, ds(i * 4, 4)].bitcast(F32), ALU.subtract).then_inc(m_done, 1)
                    first += units
                dve.wait_ge(mod_red, i + 8)
                TT(mod[:, ds(i * 8 + 56, 8)], modp, vec[:, 0, ds(i * 8 + 56, 8)], ALU.add).then_inc(mod_ready, 1)
                clear_acc()
                own.leave(4)

            own(dve.memset(sqsum[:], 0.0))
            dve.wait_ge(x_back, 16)
            dve.wait_ge(mod_ready, 11)
            with dve.Fori(0, 2) as i:
                own.enter(i, 2 * 4)
                for b in range(2):
                    par = (1 + b) % 2
                    u = Run(U_WOUT + 8 * b, i, 16)
                    a = Run(KT * 11 + 4 * b, i, 8)
                    for k in range(AHEAD, 8 + AHEAD):
                        lo(u, k)
                        if k < 8:
                            times_c(a, k - 4, i * 8 + (4 * b + k - 4))
                    dve.wait_ge(used, u.at(8))
                    for j in range(NT):
                        xt = x1[:, ds(i * 8 + (4 * b + j), 1)]
                        f = STT(out=xt, in0=ps[:, par, j:j + 1], scalar=mod[:, ds(i * 8 + (32 + 4 * b + j), 1)], in1=xt, op0=ALU.mult, op1=ALU.add)
                        if j < NT - 1:
                            own(f)
                        else:
                            f.then_inc(ps_free[par], 1)
                    dve.wait_ge(x1sq_done, i * 2 + (b + 1))
                    own(dve.tensor_reduce(sqpart[:], xsq2[:].rearrange("p a t -> p t a"), AX.X, ALU.add))
                    TT(sqsum[:], sqsum[:], sqpart[:], ALU.add).then_inc(x1sum, 1)
                own.leave(2)
            take_mod(11)
            dve.wait_ge(mod_ready, 12)
            own(STT(out=a2[:], in0=mod[:, 4 * KT:5 * KT], scalar=1.0, in1=V_G2, op0=ALU.add, op1=ALU.mult))
            dve.wait_ge(n2_rstd, 1)
            for g in range(4):
                if g:
                    dve.wait_ge(h2_ready, g)
                own(TT(xr[:], x1[:, 4 * g:4 * g + 4], rs2[:].unsqueeze(1).broadcast_to([P, 4, T]), ALU.mult))
                for j in range(4):
                    kt = 4 * g + j
                    f = TS(xr[:, j], xr[:, j], a2[:, kt:kt + 1], mod[:, 3 * KT + kt:3 * KT + kt + 1], ALU.mult, ALU.add)
                    if j < 3:
                        own(f)
                    else:
                        f.then_inc(h2f, 1)
                dve.wait_ge(h2hi_done, g + 1)
                TT(h2_lo[:, 4 * g:4 * g + 4], xr[:], h2_hi[:, 4 * g:4 * g + 4].bitcast(F32), ALU.subtract).then_inc(h2_ready, 1)

            with dve.Fori(0, UP_STEPS) as i:
                own.enter(i, 2 * (NT * 2 - 1))
                for b, cv in enumerate((cva, cvb)):
                    par = (1 + b) % 2
                    u = Run(U_UP + 8 * b, i, 16)
                    for k in range(AHEAD, 8 + AHEAD):
                        lo(u, k)
                    for j in range(NT):
                        col = i * NT + (b * FT + j)
                        dve.wait_ge(cv0, i * 8 + (4 * b + 2 * (j // 2) + 2))
                        own(STT(out=cv[:, j, 1:T], in0=ps[:, par, j, 0:T - 1], scalar=vec[:, 3, ds(col, 1)], in1=cv[:, j, 1:T], op0=ALU.mult, op1=ALU.add))
                        f = STT(out=cv[:, j, 2:T], in0=ps[:, par, j, 0:T - 2], scalar=vec[:, 2, ds(col, 1)], in1=cv[:, j, 2:T], op0=ALU.mult, op1=ALU.add)
                        if j < 3:
                            own(f)
                        else:
                            f.then_inc(ps_free[par], 1)
                dve.wait_ge(ps_free[0], i + 19)
                dve.wait_ge(sil_done, i + 1)
                TT(cvb[:], cva[:], cvb[:], ALU.mult).then_inc(gf_done, 1)
                dve.wait_ge(ghi_done, i + 1)
                TT(g_lo[:, ds(i * NT, NT)], cvb[:], g_hi[:, ds(i * NT, NT)].bitcast(F32), ALU.subtract).then_inc(g_ready, 1)
                own.leave(UP_STEPS)

            for b in range(4):
                par = (1 + b) % 2
                u = Run(U_DOWN + b * DOWN_UNITS)
                for k in range(AHEAD, DOWN_UNITS + AHEAD):
                    if u.base + k < UNITS:
                        lo(u, k)
                dve.wait_ge(used, u.at(DOWN_UNITS))
                if b >= 2:
                    dve.wait_ge(y_tr, b - 1)
                dve.wait_ge(g_ready, UP_STEPS) if b == 0 else None
                for j in range(NT):
                    kt = 4 * b + j
                    f = STT(out=ytmp[:, par, j], in0=ps[:, par, j], scalar=mod[:, 5 * KT + kt:5 * KT + kt + 1], in1=x1[:, kt], op0=ALU.mult, op1=ALU.add)
                f.then_inc(ps_free[par], 1)

        @block.tensor
        def _(pe):
            def mm(out, lhsT, rhs, start, stop=False):
                return pe.matmul(out, lhsT, rhs, start=start, stop=stop, skip_group_check=True)

            def unit(u, k, par, xh, xl, last, kind="feature"):
                pe.wait_ge(lo_done, u.at(k + 1))
                s = u.slot(k)
                for q in range(2):
                    kt = 2 * k + q
                    end = last and q == 1
                    if kind in ("feature", "keys+values"):
                        for j in range(NT if kind == "feature" else 2):
                            cols = slice(j * P, (j + 1) * P)
                            o = ps[:, par, j]
                            mm(o, w_hi[:, s, q, cols], xh[:, kt], kt == 0 and j % 2 == 0)
                            mm(o, w_hi[:, s, q, cols], xl[:, kt], False)
                            f = mm(o, w_lo[:, s, q, cols], xh[:, kt], False, end)
                    if kind == "keys+values":
                        for t in range(2):
                            o = ps[:, par, 2 + t]
                            tok = slice(t * P, (t + 1) * P)
                            mm(o, xh[:, kt, tok], w_hi[:, s, q, T:2 * T], kt == 0 and t == 0)
                            mm(o, xl[:, kt, tok], w_hi[:, s, q, T:2 * T], False)
                            f = mm(o, xh[:, kt, tok], w_lo[:, s, q, T:2 * T], False, end)
                    if kind == "token":
                        for t in range(2):
                            o = ps_tok[:, par, t]
                            tok = slice(t * P, (t + 1) * P)
                            mm(o, xh[:, kt, tok], w_hi[:, s, q], kt == 0)
                            mm(o, xl[:, kt, tok], w_hi[:, s, q], False)
                            f = mm(o, xh[:, kt, tok], w_lo[:, s, q], False, end)
                f.then_inc(used, 1)

            def free(par, n):
                pe.wait_ge(ps_free[par], n)

            def reduce_mod(chunk):
                pe.wait_ge(ada_done, (chunk + 1) * KT)
                if chunk:
                    pe.wait_ge(mod_ready, chunk)
                for j in range(ADA_COLS):
                    f = mm(b4[:, j:j + 1], acc[:, j * P:(j + 1) * P], ones[:, 0:1], True, True)
                f.then_inc(mod_red, 1)

            pe.wait_ge(consts, 1)
            pe.wait_ge(vec_in, 16 * 14)
            for n, r in enumerate((P, 118, 88, 88, 88)):
                dst = b56[:, n // 2, (n % 2) * P:(n % 2) * P + r]
                pe.transpose(dst, vrows[0:r, n, :], ident[0:r, 0:r]).then_inc(vec_tr, 1)
            pe.wait_ge(x_in, 16)
            for kt in range(KT):
                if kt < 8:
                    dst = ps[:, kt // 4, kt % 4]
                elif kt < 10:
                    dst = b4[:, (kt - 8) * T:(kt - 7) * T]
                elif kt < 14:
                    dst = b56[:, kt - 10]
                else:
                    dst = b7[:, (kt - 14) * T:(kt - 13) * T]
                if kt == 8:
                    pe.wait_ge(vec_ready, 2)
                for t in range(2):
                    f = pe.transpose(dst[:, t * P:(t + 1) * P], x_tok[:, t, kt * P:(kt + 1) * P], ident[:])
                f.then_inc(x_tr, 1)
            pe.wait_ge(misc_in, 16 * 5)
            pe.wait_ge(xT_dve, 3)
            mm(b4[:, 16:32], ones[0:1, :], snkrow[:], True, True).then_inc(snk_ps, 1)
            for kt in range(KT):
                if kt % 4 == 0:
                    pe.wait_ge(xsq_done, kt // 4 + 1)
                f = mm(b7[:, 0:T], ones[:], x_sq[:, kt], kt == 0, kt == KT - 1)
            f.then_inc(n1_sum, 1)
            pe.wait_ge(xT_act, 2)
            flat = ps[:].rearrange("p b j t -> p (b j t)")
            for j in range(P):
                f = mm(flat[:, j * HQ:(j + 1) * HQ], hot[:, P - 1 - j:2 * P - 1 - j], relt[:], True, True)
            f.then_inc(bias_ps, 1)
            pe.wait_ge(snk_ready, 1)
            for chunk in range(4):
                reduce_mod(chunk)

            def head_sums(b):
                pe.wait_ge(qk_sq, b + 1)
                f = mm(b56[:, 0:2], halves[:], sq[:, 0:2], True, True)
                if b:
                    f = mm(b56[:, 2:4], halves[:], sq[:, 2:4], True, True)
                f.then_inc(qk_sum, 1)

            pe.wait_ge(bias_sb, 2)
            for b in range(3):
                u = Run(8 * b)
                if b == 2:
                    free(0, 1)
                for k in range(8):
                    if b == 0 and k % 2 == 0:
                        pe.wait_ge(h_ready, k // 2 + 1)
                    unit(u, k, b % 2, h_hi, h_lo, k == 7, "keys+values" if b == 0 else "feature")
                    if b and k == 0:
                        head_sums(b - 1)
            pe.wait_ge(wgl_ready, 1)
            pe.wait_ge(mod_ready, 4)
            for t in range(2):
                tok = slice(t * P, (t + 1) * P)
                o = b4[:, T + t * LR:T + (t + 1) * LR]
                for kt in range(KT):
                    mm(o, h_hi[:, kt, tok], wgl_hi[:, kt], kt == 0)
                    mm(o, h_lo[:, kt, tok], wgl_hi[:, kt], False)
                    f = mm(o, h_hi[:, kt, tok], wgl_lo[:, kt], False, kt == KT - 1)
            f.then_inc(glr_ps, 1)
            head_sums(2)

            with pe.Fori(0, 2) as i:
                for b in range(2):
                    u = Run(U_GQK + 8 * b, i, 16)
                    free((1 + b) % 2, i + (1 + b))
                    for k in range(8):
                        unit(u, k, (1 + b) % 2, h_hi, h_lo, k == 7)

            pe.wait_ge(glr_sb, 1)
            for t in range(2):
                pe.transpose(b4[0:LR, T + t * P:T + (t + 1) * P], glr[:, t], ident[:]).then_inc(glrT_ps, 1)
            pe.wait_ge(glrT_sb, 1)
            reduce_mod(4)
            pe.wait_ge(qk_rstd, 3)
            for m in range(8):
                if m == 6:
                    pe.wait_ge(z_sb, 4)
                zp = b56[:, m] if m < 4 else b7[:, (m - 4) * T:(m - 3) * T] if m < 6 else b56[:, m - 6]
                mm(zp, wgk_s[:, m * P:(m + 1) * P], glrT[:], True, True).then_inc(z_ps, 1)

            pe.wait_ge(k_swapped, 32)
            pe.wait_ge(z_sb, 8)
            for g in range(4):
                par = (1 + g) % 2
                u = Run(U_GV + 8 * g)
                if g:
                    pe.wait_ge(ya_ready, g)
                else:
                    pe.wait_ge(mod_ready, 5)
                for t in range(NT):
                    half = t % 2
                    rows = slice(DH * half, DH * (half + 1))
                    q = qT[rows, 2 * g + t // 2]
                    kk = (kT if g % 2 == half else kS)[rows, g // 2]
                    mm(b56[:, 2 * half + t // 2], q[:, P:2 * P], kk, True, True)
                    o = b7[:, (t // 2) * P:(t // 2 + 1) * P] if half == 0 else b4[:, T + (t // 2) * P:T + (t // 2 + 1) * P]
                    f = mm(o, q[:, 0:P], kk[:, 0:P], True, True)
                f.then_inc(scored, 1)
                free(par, (7 + g) // 2)
                for k in range(8):
                    unit(u, k, par, h_hi, h_lo, k == 7, "token")
                pe.wait_ge(p_ready, g + 1)
                for t in range(NT):
                    pe.transpose(b7[:, t * P:(t + 1) * P], p0[:, t], ident[:])
                for kb in range(2):
                    for t in range(NT):
                        f = pe.transpose(b56[:, 2 * kb + t // 2, (t % 2) * P:(t % 2 + 1) * P], p1[:, t, kb * P:(kb + 1) * P], ident[:])
                f.then_inc(p_tr, 1)
                pe.wait_ge(pt_ready, g + 1)
                for half in range(2):
                    rows = slice(DH * half, DH * (half + 1))
                    vals = [vt[:, kb, g * DH:(g + 1) * DH] for kb in range(2)]
                    probs = [pt[:, n].rearrange("p (h q) -> p h q", q=P)[:, half:NT:2] for n in range(3)]
                    mm(b7[rows, 0:T], vals[0], probs[0], True, True)
                    mm(b7[rows, T:2 * T], vals[0], probs[1], True)
                    f = mm(b7[rows, T:2 * T], vals[1], probs[2], False, True)
                f.then_inc(pv_done, 1)
            reduce_mod(5)

            pe.wait_ge(ya_ready, 4)
            with pe.Fori(0, 2) as i:
                for b in range(2):
                    n = i * 2 + b
                    par = (1 + b) % 2
                    u = Run(U_GR + 8 * b, i, 16)
                    free(par, i + (5 + b))
                    for k in range(4):
                        unit(u, k, par, h_hi, h_lo, False)
                    pe.wait_ge(gla_ready, n + 1)
                    lo64, hi64 = slice(0, CH), slice(CH, P)
                    for rows, c0, w, keys, k0, queries, q0 in (
                            (lo64, 0, CH, ki, 0, qd, 0), (lo64, CH, CH, kx, 0, qd, CH), (lo64, 2 * CH, 2 * CH, kx, 0, qx, 0),
                            (lo64, T, CH, ki, 2 * CH, qd, 2 * CH), (lo64, T + CH, CH, kx, 2 * CH, qd, 3 * CH),
                            (hi64, CH, CH, ki, CH, qd, CH), (hi64, 2 * CH, CH, kx, CH, qd, 2 * CH), (hi64, 3 * CH, CH, kx, CH, qx, 2 * CH),
                            (hi64, T + CH, CH, ki, 3 * CH, qd, 3 * CH)):
                        for q in range(2):
                            f = mm(b7[rows, c0:c0 + w], keys[:, q, k0:k0 + CH], queries[:, q, q0:q0 + w], q == 0, q == 1)
                    f.then_inc(at_ps, 1)
                    for k in range(4, 6):
                        unit(u, k, par, h_hi, h_lo, False)
                    pe.wait_ge(at_ready, i * 4 + (2 * b + 2))
                    pe.wait_ge(gvh_ready, n + 1)
                    for j in range(NT):
                        cols = slice(j * P, (j + 1) * P)
                        mm(b56[:, j], gvh[:, 0, cols], at[:, 0:T], j % 2 == 0)
                        f = mm(b56[:, j, P:T], gvh[:, 1, cols], at[:, T:T + P], False, True)
                    f.then_inc(o_ps, 1)
                    unit(u, 6, par, h_hi, h_lo, False)
                    pe.wait_ge(osq_done, n + 1)
                    pe.wait_ge(mod_ready, 6)
                    for j in range(NT):
                        f = mm(hi_b4, ones[:], osq[:, j], j == 0, j == NT - 1)
                    f.then_inc(oss_ps, 1)
                    unit(u, 7, par, h_hi, h_lo, True)
            pe.wait_ge(rsg_ready, 4)
            reduce_mod(6)

            pe.wait_ge(yg_ready, 4)
            with pe.Fori(0, 4) as i:
                first = 0
                for b, (units, xh, xl) in enumerate(((8, h_hi, h_lo), (8, h_hi, h_lo), (4, ya_hi, ya_lo), (8, yg_hi, yg_lo))):
                    par = (1 + b) % 2
                    u = Run(U_MERGE + first, i, MERGE_UNITS)
                    free(par, i * 2 + (7 + (b + 1) // 2))
                    for k in range(units):
                        unit(u, k, par, xh, xl, k == units - 1)
                    first += units
                pe.wait_ge(ada_done, i * KT + 8 * KT)
                pe.wait_ge(mod_ready, i + 7)
                for j in range(ADA_COLS):
                    f = mm(b4[:, j:j + 1], acc[:, j * P:(j + 1) * P], ones[:, 0:1], True, True)
                f.then_inc(mod_red, 1)

            with pe.Fori(0, 2) as i:
                for b in range(2):
                    par = (1 + b) % 2
                    u = Run(U_WOUT + 8 * b, i, 16)
                    free(par, i + (15 + b))
                    for k in range(8):
                        if k >= 6:
                            pe.wait_ge(m_done, 4)
                        elif k % 2 == 0:
                            pe.wait_ge(m_done, k // 2 + 1)
                        unit(u, k, par, m_hi, m_lo, k == 7)
            reduce_mod(11)
            pe.wait_ge(x1sum, 4)
            mm(b7[:, 0:T], ones[:], sqsum[:], True, True).then_inc(n2_sum, 1)

            with pe.Fori(0, UP_STEPS) as i:
                for b in range(2):
                    par = (1 + b) % 2
                    u = Run(U_UP + 8 * b, i, 16)
                    free(par, i + (17 + b))
                    for k in range(8):
                        if b == 0 and k % 2 == 0:
                            pe.wait_ge(h2_ready, k // 2 + 1)
                        unit(u, k, par, h2_hi, h2_lo, k == 7)

            with pe.Fori(0, 2) as i:
                for b in range(2):
                    par = (1 + b) % 2
                    u = Run(U_DOWN + DOWN_UNITS * b, i, 2 * DOWN_UNITS)
                    free(par, i + (28 + b))
                    for k in range(DOWN_UNITS):
                        if b == 0 and k % 2 == 0:
                            pe.wait_ge(g_ready, k // 2 + 1)
                        unit(u, k, par, g_hi, g_lo, k == DOWN_UNITS - 1)
                    pe.wait_ge(ps_free[par], i + (29 + b))
                    for t in range(2):
                        for j in range(NT):
                            f = pe.transpose(b56[:, 2 * t + j // 2, (j % 2) * P:(j % 2 + 1) * P],
                                             ytmp[:, par, j, t * P:(t + 1) * P], ident[:])
                    f.then_inc(y_tr, 1)


_INS = ["x", "c", "rel_bias_table", "w_ada", "b_ada", "norm1_gain", "w_in", "q_norm_gain", "k_norm_gain",
        "attn_sinks", "w_gk_up", "b_gk", "gla_norm_gain", "w_branch_attn", "w_branch_gla", "w_out",
        "norm2_gain", "w_ffn_up", "ffn_conv_w", "ffn_conv_b", "w_ffn_down"]


def kernel(**inputs):
    import concourse.bacc as bacc
    from concourse.bass_utils import run_bass_kernel_spmd

    nc = bacc.Bacc("TRN2", target_bir_lowering=False, num_devices=1)
    arrays = {f"in_{name}": np.ascontiguousarray(inputs[name]) for name in _INS}
    arrays["in_onehot"] = one_hot_distances()
    args = [nc.dram_tensor(n, a.shape, mybir.dt.from_np(a.dtype), kind="ExternalInput").ap() for n, a in arrays.items()]
    out = nc.dram_tensor("out", (1, T, D), F32, kind="ExternalOutput").ap()
    layer(nc, *args, out)
    r = run_bass_kernel_spmd(nc, [arrays], core_ids=[0])
    return r.results[0]["out"]
```

```python
from contextlib import ExitStack

import numpy as np

import concourse.bass as bass
from concourse import mybir

F32 = mybir.dt.float32
F32R = mybir.dt.float32r
ALU = mybir.AluOpType
ACT = mybir.ActivationFunctionType
AX = mybir.AxisListType
ds = bass.ds

P = 128
D = 2048
T = 256
KT = D // P
NB = 512
NT = NB // P
HQ, HKV, DH = 16, 4, 64
NBUCKETS, MAXDIST = 32, 128
GH, DK, DV, LR, CH = 4, 256, 512, 16, 64
FF = 5632
FT = FF // P
D_IN = 11792
EPS = 1e-6
MASKED = -1e30

C_AQ, C_AKV, C_GQ, C_GV, C_GR, C_GLR = 0, 1024, 1536, 3584, 5632, 7680
C_GA, C_GB = 7696, 9744

SLOTS = 4
AHEAD = 4
ADA_SLOTS = 4
ADA_W = 1024
ADA_COLS = ADA_W // P

U_GQK = 24
U_GV = 56
U_GR = 88
U_MERGE = 120
MERGE_UNITS = 8 + 8 + 4 + 8
U_WOUT = U_MERGE + 4 * MERGE_UNITS
U_UP = U_WOUT + 32
UP_STEPS = FF // NB
U_DOWN = U_UP + 16 * UP_STEPS
DOWN_UNITS = FT // 2
UNITS = U_DOWN + 4 * DOWN_UNITS

QK_STEPS = ((16, 20, 16), (20, 24, 20), (24, 28, 24))

MOD_TILE = (0, 16, 8, 24, 32, 40, 48, 56, 64, 72, 80, 88)


def one_hot_distances():
    dist = P - 1 - np.arange(P)
    half = NBUCKETS // 2
    large = half + (np.log(np.maximum(dist, 1) / half) / np.log(MAXDIST / half) * (NBUCKETS - half)).astype(np.int64)
    bucket = np.where(dist < half, dist, np.minimum(large, NBUCKETS - 1))
    return (np.arange(NBUCKETS)[:, None] == bucket[None, :]).astype(np.float32)


class Run:

    def __init__(self, base, i=None, per=0):
        self.base, self.i, self.per = base, i, per

    def at(self, k=0):
        return self.base + k if self.i is None else self.i * self.per + (self.base + k)

    def slot(self, k):
        return (self.base + k) % SLOTS

    def landed(self, k):
        n = 16 * ((self.base + k) // SLOTS + 1)
        return n if self.i is None else self.i * (16 * self.per // SLOTS) + n


class Own:

    def __init__(self, eng, sem):
        self.eng, self.sem, self.n, self.i, self.per = eng, sem, 0, None, 0

    def __call__(self, instruction):
        instruction.then_inc(self.sem, 1)
        self.n += 1
        self.eng.wait_ge(self.sem, self.n if self.i is None else self.i * self.per + self.n)

    def note(self, instruction):
        instruction.then_inc(self.sem, 1)
        self.n += 1

    def enter(self, i, per):
        self.i, self.per, self.start = i, per, self.n

    def leave(self, turns):
        assert self.n - self.start == self.per, (self.n - self.start, self.per)
        self.n, self.i = self.start + turns * self.per, None


def layer(nc, x, c, rel, w_ada, b_ada, g1, w_in, qg, kg, sinks, wgk, bgk, ggla, wba, wbg, wo, g2,
          w_up, conv_w, conv_b, w_dn, onehot, out):
    xs = nc.dram_tensor("x_featuremajor", (P, KT, T), F32, kind="Internal").ap()
    rel_dram = nc.dram_tensor("bias_by_distance", (HQ, P + 1, P), F32, kind="Internal").ap()
    w_in_u = w_in[0].rearrange("(u k p) n -> u p k n", k=2, p=P)
    wba_u = wba[0].rearrange("(u k p) n -> u p k n", k=2, p=P)
    wbg_u = wbg[0].rearrange("(u k p) n -> u p k n", k=2, p=P)
    wo_u = wo[0].rearrange("(u k p) n -> u p k n", k=2, p=P)
    up_u = w_up[0].rearrange("(u k p) n -> u p k n", k=2, p=P)
    dn_u = w_dn[0].rearrange("(u k p) n -> u p k n", k=2, p=P)
    ada_k = w_ada[0].rearrange("(k p) n -> p k n", p=P)
    out_t = out[0].rearrange("(t p) n -> p t n", p=P)

    KB = 1024
    base = 16512

    def sb(name, at, shape, dt=F32):
        return nc.alloc_sbuf_tensor_at(name, shape, dt, offset=base + int(at * KB))

    h_hi = sb("h_hi", 0, [P, KT, T], F32R)
    h_lo = sb("h_lo", 16, [P, KT, T], F32R)
    x1 = sb("x1", 0, [P, KT, T])
    h2_hi = sb("h2_hi", 16, [P, KT, T], F32R)
    h2_lo = sb("h2_lo", 32, [P, KT, T], F32R)
    xT = sb("xT", 32, [P, KT, T])
    gv = sb("gv", 32, [P, GH, 2, DV])
    yg_lo = sb("yg_lo", 32, [P, KT, T], F32R)
    bias = sb("bias", 48, [P, HQ, 2 * P])
    yg_hi = sb("yg_hi", 48, [P, KT, T], F32R)
    x_sq = sb("x_sq", 64, [P, KT, T])
    xn = sb("xn", 64, [P, KT, T])
    ya_hi = sb("ya_hi", 64, [P, 8, T], F32R)
    ya_lo = sb("ya_lo", 72, [P, 8, T], F32R)
    x_tok = sb("x_tok", 80, [P, 2, D])
    gqk = sb("gqk", 80, [P, 2 * 8, T])
    m_hi = sb("m_hi", 80, [P, KT, T], F32R)
    vrows = sb("vrows", 96, [P, 5, P])
    lg = sb("lg", 96, [P, 8, T])
    sig_a = sb("sig_a", 96, [P, NT, T])
    sig_b = sb("sig_b", 100, [P, NT, T])
    qT = sb("qT", 104, [P, 8, T])
    hot = sb("hot", 104, [NBUCKETS, P])
    relt = sb("relt", 106, [NBUCKETS, HQ])
    rel_rows = sb("rel_rows", 80, [HQ, P])
    kT = sb("kT", 112, [P, 2, T])
    kS = sb("kS", 114, [P, 2, T])
    vt = sb("vt", 116, [P, 2, 2 * P])
    sq = sb("sq", 118, [P, NT, T])
    rstd = sb("rstd", 122, [P, NT, T])
    p1 = sb("p1", 118, [P, NT, 2 * P])
    p0 = sb("p0", 122, [P, NT, P])
    pt = sb("pt", 124, [P, 3, NB])
    wgl = sb("wgl", 126, [P, KT, LR])
    wgl_hi = sb("wgl_hi", 127, [P, KT, LR], F32R)
    wgl_lo = sb("wgl_lo", 128, [P, KT, LR], F32R)
    glr = sb("glr", 129, [P, 2, LR])
    glrT = sb("glrT", 129.25, [LR, T])
    lnp = sb("lnp", 130, [P, 2, T])
    wgk_s = sb("wgk_s", 132, [LR, 8 * P])
    m_lo = sb("m_lo", 104, [P, KT, T], F32R)
    eg = sb("eg", 104, [P, 2, T])
    en = sb("en", 106, [P, 2, T])
    kx = sb("kx", 108, [P, 2, 3 * CH])
    qx = sb("qx", 109.5, [P, 2, 3 * CH])
    qd = sb("qd", 111, [P, 2, T])
    ki = sb("ki", 113, [P, 2, T])
    gvh = sb("gvh", 117, [P, 2, DV])
    osq = sb("osq", 121, [P, NT, T])
    sil = sb("sil", 125, [P, NT, T])
    yt = sb("yt", 129, [P, NT, T])
    rsg = sb("rsg", 133, [P, T])
    mrg = sb("mrg", 120, [P, NT, T])
    mrg2 = sb("mrg2", 124, [P, NT, T])
    xsq2 = sb("xsq2", 120, [P, NT, T])
    sqsum = sb("sqsum", 134, [P, 2, T])
    rs2 = sb("rs2", 126, [P, T])
    xr = sb("xr", 128, [P, NT, T])
    g_hi = sb("g_hi", 48, [P, FT, T], F32R)
    g_lo = sb("g_lo", 92, [P, FT, T], F32R)
    stage = sb("stage", 136, [P, SLOTS, 2, NB])
    w_hi = sb("w_hi", 152, [P, SLOTS, 2, NB], F32R)
    w_lo = sb("w_lo", 168, [P, SLOTS, 2, NB], F32R)
    ada = sb("ada", 184, [P, ADA_SLOTS, ADA_W])
    acc = sb("acc", 200, [P, ADA_W])
    acc_odd = sb("acc_odd", 99, [P, ADA_W])
    cva = sb("cva", 184, [P, NT, T])
    cvb = sb("cvb", 188, [P, NT, T])
    ytmp = sb("ytmp", 184, [P, 2, NT, T])
    outs = sb("outs", 192, [P, 2, 2, NB])
    ident = sb("ident", 204, [P, P])
    ones = sb("ones", 204.5, [P, P])
    vec = sb("vec", 205, [P, 5, P])

    def small(name, row, col, shape):
        return sb(name, 205 + (row * P + col) * 4 / KB, shape)

    a1, a2 = small("a1", 2, 88, [P, KT]), small("a2", 2, 104, [P, KT])
    cact, snk = small("cact", 3, 88, [P, KT]), small("snk", 3, 104, [P, HQ])
    mx, nmx = small("mx", 4, 88, [P, 2, NT]), small("nmx", 4, 96, [P, 2, NT])
    esk, rsum = small("esk", 4, 104, [P, 2, NT]), small("rsum", 4, 112, [P, 2, NT])
    eps = small("eps", 1, 120, [P, 8])
    mod = small("mod", 4, 120, [P, 96])
    snkrow = sb("snkrow", 131.25, [1, HQ])
    halves = sb("halves", 130.5, [P, P])
    keep = sb("keep", 133, [P, T])
    at = sb("at", 115, [P, 384])

    ps = nc.alloc_psum_tensor("ps", [P, 2, NT, T], F32)
    b4 = nc.alloc_psum_tensor("b4", [P, NB], F32)
    b56 = nc.alloc_psum_tensor("b56", [P, NT, T], F32)
    b7 = nc.alloc_psum_tensor("b7", [P, NB], F32)
    ps_tok = ps[:].rearrange("p b j t -> p b (j t)").rearrange("p b (a n) -> p b a n", a=2)
    modp = b4[:, 0:ADA_COLS]
    hi_b4 = b4[:, T:2 * T]

    V_BADA = vec[:, 0, 0:96]
    V_G1 = vec[:, 0, 96:112]
    V_C = vec[:, 0, 112:128]
    V_G2 = vec[:, 1, 88:104]
    V_BGK = vec[:, 1, 104:112]
    V_GG = vec[:, 1, 112:116]
    V_QG = vec[:, 1, 116:117]
    V_KG = vec[:, 1, 117:118]

    with ExitStack() as ctx:
        def sem(name):
            return ctx.enter_context(nc.semaphore(name))

        stage_full = [sem(f"stage_full{i}") for i in range(SLOTS)]
        ada_full = [sem(f"ada_full{i}") for i in range(ADA_SLOTS)]
        hi_done = sem("hi_done")
        lo_done = sem("lo_done")
        used = sem("used")
        ps_free = [sem("ps_free0"), sem("ps_free1")]
        ada_done = sem("ada_done")
        mod_red = sem("mod_red")
        mod_ready = sem("mod_ready")
        vec_in, x_in, misc_in = sem("vec_in"), sem("x_in"), sem("misc_in")
        consts, keep_ready = sem("consts"), sem("keep_ready")
        vec_tr, vec_ready = sem("vec_tr"), sem("vec_ready")
        x_tr, xT_act, xT_dve, xs_out = sem("x_tr"), sem("xT_act"), sem("xT_dve"), sem("xs_out")
        xsq_done, n1_sum, n1_rstd = sem("xsq_done"), sem("n1_sum"), sem("n1_rstd")
        cact_ready = sem("cact_ready")
        rel_ps, rel_sb, rel_out, bias_in, bias_ready = (
            sem("rel_ps"), sem("rel_sb"), sem("rel_out"), sem("bias_in"), sem("bias_ready"))
        snk_ps, snk_ready = sem("snk_ps"), sem("snk_ready")
        wgl_hi_done, wgl_ready = sem("wgl_hi_done"), sem("wgl_ready")
        hf_done, hhi_done, h_ready = sem("hf_done"), sem("hhi_done"), sem("h_ready")
        qk_sq, qk_sum, qk_rstd, k_ready, k_swapped = (
            sem("qk_sq"), sem("qk_sum"), sem("qk_rstd"), sem("k_ready"), sem("k_swapped"))
        scored, m_ready, exped, p_ready = sem("scored"), sem("m_ready"), sem("exped"), sem("p_ready")
        p_tr, pt_ready, pv_done, yahi_done, ya_ready = (
            sem("p_tr"), sem("pt_ready"), sem("pv_done"), sem("yahi_done"), sem("ya_ready"))
        glr_ps, glr_sb, glrT_ps, glrT_sb, z_ps, z_sb = (
            sem("glr_ps"), sem("glr_sb"), sem("glrT_ps"), sem("glrT_sb"), sem("z_ps"), sem("z_sb"))
        lnp_ready, lg_ready = sem("lnp_ready"), sem("lg_ready")
        gla_arg, gla_exp, gla_ready = sem("gla_arg"), sem("gla_exp"), sem("gla_ready")
        at_ps, at_sb, at_ready, gvh_ready = sem("at_ps"), sem("at_sb"), sem("at_ready"), sem("gvh_ready")
        at_zero = sem("at_zero")
        o_ps, osq_done, osq_sum, oss_ps, rsg_ready = sem("o_ps"), sem("osq_done"), sem("osq_sum"), sem("oss_ps"), sem("rsg_ready")
        yt_ready, yghi_done, yg_ready = sem("yt_ready"), sem("yghi_done"), sem("yg_ready")
        mrg_ready, mhi_done, m_done = sem("mrg_ready"), sem("mhi_done"), sem("m_done")
        x_back, x1_done, x1sq_done = sem("x_back"), sem("x1_done"), sem("x1sq_done")
        n2_sum, n2_rstd, h2f, h2hi_done, h2_ready = (
            sem("n2_sum"), sem("n2_rstd"), sem("h2f"), sem("h2hi_done"), sem("h2_ready"))
        cv0, sil_done, gf_done, ghi_done, g_ready = (
            sem("cv0"), sem("sil_done"), sem("gf_done"), sem("ghi_done"), sem("g_ready"))
        out_half, down_half = sem("out_half"), sem("down_half")
        y_tile, y_tr, outs_ready, stored = sem("y_tile"), sem("y_tr"), sem("outs_ready"), sem("stored")
        act_own, dve_own, pool_own = sem("act_own"), sem("dve_own"), sem("pool_own")

        block = ctx.enter_context(nc.Block())

        @block.sync
        def _(sp):
            def load(u, k, src):
                if u.base + k >= SLOTS:
                    sp.wait_ge(lo_done, u.at(k - SLOTS + 1))
                sp.dma_start(stage[:, u.slot(k)], src).then_inc(stage_full[u.slot(k)], 16)

            def load_ada(a, k, kt, col):
                if a.base + k >= ADA_SLOTS:
                    sp.wait_ge(ada_done, a.at(k - ADA_SLOTS + 1))
                src = ada_k[:, kt, col] if isinstance(kt, int) else ada_k[:, ds(kt, 1), col].rearrange("p k n -> p (k n)")
                sp.dma_start(ada[:, a.slot(k)], src).then_inc(ada_full[a.slot(k)], 16)

            def store(b):
                sp.wait_ge(outs_ready, b + 1)
                sp.dma_start(out_t[:, :, b * NB:(b + 1) * NB], outs[:, b % 2]).then_inc(stored, 16)

            def rows(dram, n):
                return dram.rearrange("(r f) -> r f", f=n)

            sp.dma_start(vrows[0:96, 0, :], rows(b_ada[0], P)).then_inc(vec_in, 16)
            sp.dma_start(vrows[96:112, 0, :], rows(g1[0], P)).then_inc(vec_in, 16)
            sp.dma_start(vrows[112:128, 0, :], rows(c[0], P)).then_inc(vec_in, 16)
            sp.dma_start(x_tok[:], x[0].rearrange("(t p) n -> p t n", p=P)).then_inc(x_in, 16)
            sp.dma_start(vrows[0:88, 1, :], rows(conv_b[0], P)).then_inc(vec_in, 16)
            sp.dma_start(vrows[88:104, 1, :], rows(g2[0], P)).then_inc(vec_in, 16)
            sp.dma_start(vrows[104:112, 1, :], rows(bgk[0], P)).then_inc(vec_in, 16)
            sp.dma_start(vrows[112:116, 1, :], rows(ggla[0], P)).then_inc(vec_in, 16)
            for half in range(2):
                cols = slice(half * DH, (half + 1) * DH)
                sp.dma_start(vrows[116:117, 1, cols], qg).then_inc(vec_in, 16)
                sp.dma_start(vrows[117:118, 1, cols], kg).then_inc(vec_in, 16)
            for tap in range(3):
                sp.dma_start(vrows[0:88, 2 + tap, :], rows(conv_w[0, tap], P)).then_inc(vec_in, 16)
            sp.dma_start(relt[:], rel).then_inc(misc_in, 16)
            sp.dma_start(hot[:], onehot).then_inc(misc_in, 16)
            sp.dma_start(snkrow[:], sinks).then_inc(misc_in, 16)
            sp.dma_start(wgl[:], w_in[0, :, C_GLR:C_GLR + LR].rearrange("(k p) n -> p k n", p=P)).then_inc(misc_in, 16)
            sp.dma_start(wgk_s[:], wgk[0]).then_inc(misc_in, 16)

            u = Run(0)

            def load_half(half, b, k):
                col = (C_AKV, C_AQ, C_AQ + NB)[b]
                load(u, 12 * half + 4 * b + k, w_in_u[4 * half + k][:, :, col:col + NB])

            for k in range(4):
                load_half(0, 0, k)
            a = Run(0)
            for n in range(4 * KT):
                col = MOD_TILE[n // KT] * P
                load_ada(a, n, n % KT, slice(col, col + ADA_W))
                if n in (30, 32, 34, 36):
                    load_half(0, 1, (n - 30) // 2)
                if n in (44, 46, 48, 50):
                    load_half(0, 2, (n - 44) // 2)
            for k in range(4):
                load_half(1, 0, k)
            sp.wait_ge(rel_sb, 1)
            sp.dma_start(rel_dram, rel_rows[:].unsqueeze(1).broadcast_to([HQ, P + 1, P])).then_inc(rel_out, 16)
            sp.wait_ge(xT_act, 2)
            sp.wait_ge(xT_dve, 3)
            sp.dma_start(xs, xT[:]).then_inc(xs_out, 16)
            for k in range(4):
                load_half(1, 1, k)
            for k in range(2):
                load_half(1, 2, k)
            sp.wait_ge(k_ready, 1)
            sp.dma_start(kS[0:DH], kT[DH:P]).then_inc(k_swapped, 16)
            sp.dma_start(kS[DH:P], kT[0:DH]).then_inc(k_swapped, 16)
            for k in range(2, 4):
                load_half(1, 2, k)
            sp.wait_ge(rel_out, 16)
            by_query = bass.AP(rel_dram.tensor, P - 1, [[P - 1, P], [(P + 1) * P, HQ], [1, 2 * P]])
            sp.dma_start(bias[:], by_query).then_inc(bias_in, 16)

            def two_by_two(unit0, views, col0, chunk):
                with sp.Fori(0, 2) as i:
                    for b in range(2):
                        u = Run(unit0 + 8 * b, i, 16)
                        a = Run(KT * chunk + 4 * b, i, 8)
                        for k in range(8):
                            load(u, k, views[k][:, :, ds(i * (2 * NB) + (col0 + b * NB), NB)])
                            if k >= 4:
                                load_ada(a, k - 4, i * 8 + (4 * b + k - 4), slice(chunk * ADA_W, (chunk + 1) * ADA_W))

            two_by_two(U_GQK, w_in_u, C_GQ, 4)
            two_by_two(U_GV, w_in_u, C_GV, 5)
            two_by_two(U_GR, w_in_u, C_GR, 6)

            with sp.Fori(1, 5) as i:
                n0 = i * NB - NB
                a = Run(KT * 6, i, KT)
                kt = 0
                first = 0
                for src, units, col0, extra in ((w_in_u, 8, C_GA, (1, 1, 1, 2)), (w_in_u, 8, C_GB, (1, 1, 1, 2)),
                                                (wba_u, 4, 0, ()), (wbg_u, 8, 0, (1, 2, 1, 2))):
                    u = Run(U_MERGE - MERGE_UNITS + first, i, MERGE_UNITS)
                    for k in range(units):
                        load(u, k, src[k][:, :, ds(n0 + col0, NB)])
                        for _ in range(extra[k - 4] if k >= 4 and extra else 0):
                            load_ada(a, kt, kt, ds(i * ADA_W + 6 * ADA_W, ADA_W))
                            kt += 1
                    first += units

            sp.wait_ge(used, U_WOUT - 12)
            sp.wait_ge(xs_out, 16)
            sp.dma_start(x1[:], xs).then_inc(x_back, 16)
            two_by_two(U_WOUT, wo_u, 0, 11)

            with sp.Fori(0, UP_STEPS) as i:
                for b in range(2):
                    u = Run(U_UP + 8 * b, i, 16)
                    for k in range(8):
                        load(u, k, up_u[k][:, :, ds(i * NB + b * FF, NB)])

            for b in range(4):
                for k in range(DOWN_UNITS):
                    load(Run(U_DOWN + b * DOWN_UNITS), k, dn_u[k][:, :, b * NB:(b + 1) * NB])
                    if b and k == 8:
                        store(b - 1)
            store(3)
            sp.wait_ge(stored, 16 * 4)

        @block.gpsimd
        def _(pool):
            own = Own(pool, pool_own)

            own(pool.memset(ident[:], 1.0))
            own(pool.affine_select(out=ident[:], in_=ident[:], compare_op=ALU.is_equal, fill=0.0, base=0,
                                   pattern=[[-1, P]], channel_multiplier=1))
            own(pool.memset(ones[:], 1.0))
            own(pool.memset(halves[:], 0.0))
            own(pool.memset(halves[0:DH, 0:DH], 1.0))
            own(pool.memset(halves[DH:P, DH:P], 1.0))
            pool.memset(eps[:], EPS).then_inc(consts, 1)
            for k in range(16):
                pool.wait_ge(hi_done, k + 1)
                pool.tensor_tensor(w_lo[:, k % SLOTS], stage[:, k % SLOTS], w_hi[:, k % SLOTS].bitcast(F32), ALU.subtract).then_inc(lo_done, 1)
            pool.wait_ge(consts, 1)
            pool.wait_ge(bias_in, 16)
            pool.affine_select(out=bias[:, :, P:2 * P], in_=bias[:, :, P:2 * P], compare_op=ALU.is_ge, fill=MASKED,
                               base=0, pattern=[[0, HQ], [-1, P]], channel_multiplier=1).then_inc(bias_ready, 1)
            pool.wait_ge(bias_ready, 1)
            pool.affine_select(out=bias[:, :, 0:P], in_=bias[:, :, 0:P], compare_op=ALU.is_gt, fill=MASKED,
                               base=0, pattern=[[0, HQ], [1, P]], channel_multiplier=-1).then_inc(bias_ready, 1)
            pool.wait_ge(bias_ready, 2)
            pool.wait_ge(z_sb, 8)
            own(pool.memset(keep[:], 1.0))
            pool.memset(keep[:].rearrange("p (c t) -> p c t", t=CH)[:, :, 0:1], 0.0).then_inc(keep_ready, 1)
            pool.wait_ge(keep_ready, 1)
            pool.wait_ge(pv_done, 4)
            pool.wait_ge(p_ready, 4)
            pool.wait_ge(ps_free[0], 6)
            pool.wait_ge(ps_free[1], 5)
            pool.memset(at[:], 0.0).then_inc(at_zero, 1)
            pool.wait_ge(at_zero, 1)
            for h in range(GH):
                if h:
                    pool.wait_ge(o_ps, h)
                    pool.wait_ge(at_ready, 2 * h)
                pool.tensor_copy(gvh[:].rearrange("p a n -> p (a n)"),
                                 gv[:, h].rearrange("p a n -> p (a n)")).then_inc(gvh_ready, 1)
                pool.wait_ge(gvh_ready, h + 1)
                pool.wait_ge(at_sb, h + 1)
                pool.affine_select(out=at[:, 0:T], in_=at[:, 0:T], compare_op=ALU.is_ge, fill=0.0, base=0,
                                   pattern=[[1, T]], channel_multiplier=-1).then_inc(at_ready, 1)
                pool.wait_ge(at_ready, 2 * h + 1)
                pool.affine_select(out=at[:, T:T + P], in_=at[:, T:T + P], compare_op=ALU.is_ge, fill=0.0, base=0,
                                   pattern=[[1, P]], channel_multiplier=-1).then_inc(at_ready, 1)
                pool.wait_ge(osq_done, h + 1)
                own(pool.tensor_tensor(osq[:, 0:2], osq[:, 0:2], osq[:, 2:4], ALU.add))
                pool.tensor_tensor(osq[:, 0], osq[:, 0], osq[:, 1], ALU.add).then_inc(osq_sum, 1)

        @block.scalar
        def _(act):
            own = Own(act, act_own)

            def hi(u, k):
                act.wait_ge(stage_full[u.slot(k)], u.landed(k))
                if u.base + k >= SLOTS:
                    act.wait_ge(used, u.at(k - SLOTS + 1))
                act.activation(w_hi[:, u.slot(k)], stage[:, u.slot(k)], ACT.Copy).then_inc(hi_done, 1)

            def rstd_of(dst, src, n):
                own(act.activation(dst, src, ACT.Ln, scale=1.0 / n, bias=eps[:, 0:1]))
                return act.activation(dst, dst, ACT.Exp, scale=-0.5)

            def results_out(b):
                act.wait_ge(y_tr, b + 1)
                if b >= 2:
                    act.wait_ge(stored, 16 * (b - 1))
                act.activation(outs[:, b % 2], b56[:].rearrange("p (a j) t -> p a (j t)", a=2), ACT.Copy).then_inc(outs_ready, 1)

            act.wait_ge(vec_ready, 1)
            act.activation(cact[:], V_C, ACT.Silu).then_inc(cact_ready, 1)
            for b in range(2):
                act.wait_ge(x_tr, 4 * (b + 1))
                act.activation(xT[:, 4 * b:4 * b + 4], ps[:, b], ACT.Copy).then_inc(xT_act, 1)
            act.wait_ge(xT_act, 2)
            act.wait_ge(xT_dve, 3)
            for b in range(4):
                act.activation(x_sq[:, 4 * b:4 * b + 4], xT[:, 4 * b:4 * b + 4], ACT.Square).then_inc(xsq_done, 1)
            u = Run(0)
            for k in range(4):
                hi(u, k)
            act.wait_ge(consts, 1)
            act.wait_ge(n1_sum, 1)
            rstd_of(rstd[:, 0], b7[:, 0:T], D).then_inc(n1_rstd, 1)
            act.wait_ge(misc_in, 16 * 5)
            act.activation(wgl_hi[:], wgl[:], ACT.Copy).then_inc(wgl_hi_done, 1)
            act.wait_ge(rel_ps, 1)
            act.activation(rel_rows[:], b56[0:HQ, 0, 0:P], ACT.Copy).then_inc(rel_sb, 1)

            def h_hi_of(pair):
                act.wait_ge(hf_done, pair + 1)
                for kt in (2 * pair, 2 * pair + 1):
                    f = act.activation(h_hi[:, kt], xn[:, kt], ACT.Identity, bias=mod[:, kt:kt + 1])
                f.then_inc(hhi_done, 1)

            for pair in range(4):
                h_hi_of(pair)
            for k in range(4, 12):
                hi(u, k)
            for pair in range(4, 8):
                hi(u, 8 + pair)
                h_hi_of(pair)

            for b, (first, end, done) in enumerate(QK_STEPS):
                for k in range(first, end):
                    hi(u, k)
                tiles = 2 if b == 0 else 4
                act.wait_ge(used, done)
                if b:
                    act.wait_ge(ps_free[(b - 1) % 2], 1)
                act.activation(sq[:, 0:tiles], (ps[:, 0, 0:2], ps[:, 1], b56[:])[b], ACT.Square).then_inc(qk_sq, 1)
                act.wait_ge(qk_sum, b + 1)
                sums = ps[:, 0] if b else b7[:].rearrange("p (j t) -> p j t", j=2)
                rstd_of(rstd[:, 0:tiles], sums, DH).then_inc(qk_rstd, 1)

            with act.Fori(0, 2) as i:
                for b in range(2):
                    u = Run(U_GQK + 8 * b, i, 16)
                    for k in range(AHEAD, 8 + AHEAD):
                        hi(u, k)

            def decays(h):
                act.activation(eg[:], lg[:, 2 * h:2 * h + 2], ACT.Exp, scale=1 / 16).then_inc(gla_exp, 1)
                act.activation(en[:], lg[:, 2 * h:2 * h + 2], ACT.Exp, scale=-1 / 16).then_inc(gla_exp, 1)

            def cross_decays(h):
                act.wait_ge(gla_arg, h + 1)
                act.activation(kx[:], kx[:], ACT.Exp, scale=1 / 16).then_inc(gla_exp, 1)
                act.activation(qx[:], qx[:], ACT.Exp, scale=1 / 16).then_inc(gla_exp, 1)

            def probs_out(g):
                act.wait_ge(p_tr, g + 1)
                own(act.activation(pt[:, 0], b7[:], ACT.Copy))
                act.activation(pt[:, 1:3], b56[:], ACT.Copy).then_inc(pt_ready, 1)

            def attended_hi(g):
                act.wait_ge(pv_done, g + 1)
                act.activation(ya_hi[:, 2 * g:2 * g + 2].rearrange("p t (n q) -> p t n q", n=2),
                               b7[:].rearrange("p (n t q) -> p t n q", n=2, t=2), ACT.Copy).then_inc(yahi_done, 1)

            for g in range(4):
                u = Run(U_GV + 8 * g)
                hi(u, 4)
                if g == 0:
                    for m in range(8):
                        act.wait_ge(z_ps, m // 2 * 2 + 2)
                        zp = b56[:, m] if m < 4 else b7[:, (m - 4) * T:(m - 3) * T] if m < 6 else b56[:, m - 6]
                        act.activation(lg[:, m], zp, ACT.Identity, bias=V_BGK[:, m:m + 1]).then_inc(z_sb, 1)
                    act.wait_ge(z_sb, 8)
                hi(u, 5)
                if g:
                    probs_out(g - 1)
                    act.wait_ge(lg_ready, g)
                own(act.activation(lnp[:], lg[:, 2 * g:2 * g + 2], ACT.Abs))
                own(act.activation(lnp[:], lnp[:], ACT.Exp, scale=-1.0))
                act.activation(lnp[:], lnp[:], ACT.Ln, bias=1.0).then_inc(lnp_ready, 1)
                hi(u, 6)
                if g:
                    attended_hi(g - 1)
                hi(u, 7)
                hi(u, 8)
                act.wait_ge(m_ready, g + 1)
                for t in range(NT):
                    own(act.activation(p0[:, t], p0[:, t], ACT.Exp, bias=nmx[:, 0, t:t + 1], accum_out=rsum[:, 0, t:t + 1]))
                if g < 3:
                    hi(u, 9)
                for t in range(NT):
                    own(act.activation(p1[:, t], p1[:, t], ACT.Exp, bias=nmx[:, 1, t:t + 1], accum_out=rsum[:, 1, t:t + 1]))
                act.activation(esk[:], esk[:], ACT.Exp).then_inc(exped, 1)
                for k in range(10 if g < 3 else 9, 12):
                    hi(u, k)
            act.wait_ge(lg_ready, 4)
            decays(0)
            probs_out(3)
            attended_hi(3)
            cross_decays(0)

            act.wait_ge(p_ready, 4)
            for n in range(GH):
                u = Run(U_GR + 8 * n)
                hi(u, 4)
                hi(u, 5)
                act.wait_ge(at_zero, 1)
                act.wait_ge(at_ps, n + 1)
                own(act.activation(at[0:CH, 0:T], b7[0:CH, 0:T], ACT.Copy))
                own(act.activation(at[CH:P, CH:T], b7[CH:P, CH:T], ACT.Copy))
                own(act.activation(at[0:CH, T:T + P], b7[0:CH, T:T + P], ACT.Copy))
                act.activation(at[CH:P, T + CH:T + P], b7[CH:P, T + CH:T + P], ACT.Copy).then_inc(at_sb, 1)
                hi(u, 6)
                if n < GH - 1:
                    decays(n + 1)
                hi(u, 7)
                if n < GH - 1:
                    cross_decays(n + 1)
                hi(u, 8)
                act.wait_ge(o_ps, n + 1)
                act.activation(osq[:], b56[:], ACT.Square).then_inc(osq_done, 1)
                hi(u, 9)
                act.wait_ge(oss_ps, n + 1)
                rstd_of(rsg[:], hi_b4, DV).then_inc(rsg_ready, 1)
                hi(u, 10)
                hi(u, 11)
                act.wait_ge(used, u.at(8))
                act.activation(sil[:], ps[:, (1 + n) % 2], ACT.Silu).then_inc(ps_free[(1 + n) % 2], 1)
                act.wait_ge(yt_ready, n + 1)
                act.activation(yg_hi[:, 4 * n:4 * n + 4], yt[:], ACT.Copy).then_inc(yghi_done, 1)

            own(act.activation(eps[:, 1:2], eps[:, 0:1], ACT.Sigmoid))
            with act.Fori(0, 4) as i:
                first = 0
                for b, (units, sig) in enumerate(((8, sig_a), (8, sig_b), (4, None), (8, None))):
                    u = Run(U_MERGE + first, i, MERGE_UNITS)
                    for k in range(AHEAD, units + AHEAD):
                        hi(u, k)
                    if sig is not None:
                        act.wait_ge(used, u.at(units))
                        act.activation(sig[:], ps[:, (1 + b) % 2], ACT.Sigmoid).then_inc(ps_free[(1 + b) % 2], 1)
                    first += units
                act.wait_ge(mrg_ready, i + 1)
                act.activation(m_hi[:, ds(i * 4, 4)], mrg[:], ACT.Copy).then_inc(mhi_done, 1)

            with act.Fori(0, 2) as i:
                for b in range(2):
                    u = Run(U_WOUT + 8 * b, i, 16)
                    for k in range(AHEAD, 7 + AHEAD):
                        hi(u, k)
                    for half in range(2):
                        act.wait_ge(x1_done, i * 4 + (2 * b + half + 1))
                        act.activation(xsq2[:, 2 * half:2 * half + 2], x1[:, ds(i * 8 + (4 * b + 2 * half), 2)], ACT.Square).then_inc(x1sq_done, 1)
                    hi(u, 7 + AHEAD)
            own(act.activation(eps[:, 1:2], eps[:, 0:1], ACT.Ln))
            act.wait_ge(n2_sum, 1)
            rstd_of(rs2[:], b7[:, 0:T], D).then_inc(n2_rstd, 1)
            for pair in range(8):
                act.wait_ge(h2f, pair + 1)
                for j in range(2):
                    kt = 2 * pair + j
                    f = act.activation(h2_hi[:, kt], xr[:, kt % 4], ACT.Identity, bias=mod[:, 3 * KT + kt:3 * KT + kt + 1])
                f.then_inc(h2hi_done, 1)

            for k in range(AHEAD, 8 + AHEAD):
                hi(Run(U_UP), k)
            own(act.activation(eps[:, 1:2], eps[:, 0:1], ACT.Silu))
            with act.Fori(0, UP_STEPS) as i:
                for b, cv in enumerate((cva, cvb)):
                    u = Run(U_UP + 8 * b, i, 16)
                    act.wait_ge(used, u.at(8))
                    for k in range(8):
                        if k < 2:
                            for j in (2 * k, 2 * k + 1):
                                col = i * NT + (b * FT + j)
                                act.activation(cv[:, j], ps[:, (1 + b) % 2, j], ACT.Identity,
                                               scale=vec[:, 4, ds(col, 1)], bias=vec[:, 1, ds(col, 1)]).then_inc(cv0, 1)
                        hi(u, 8 + AHEAD + k)
                        if k == 3 and b == 0:
                            act.wait_ge(ps_free[1], i + 18)
                            act.activation(cva[:], cva[:], ACT.Silu).then_inc(sil_done, 1)
                        if k == 4 and b == 1:
                            act.wait_ge(gf_done, i + 1)
                            act.activation(g_hi[:, ds(i * NT, NT)], cvb[:], ACT.Copy).then_inc(ghi_done, 1)

            for b in range(4):
                u = Run(U_DOWN + b * DOWN_UNITS)
                for k in range(8 + AHEAD if b == 0 else AHEAD, DOWN_UNITS + AHEAD):
                    if u.base + k < UNITS:
                        hi(u, k)
                    if b and k == 8:
                        results_out(b - 1)
            results_out(3)

        @block.vector
        def _(dve):
            own = Own(dve, dve_own)
            TT, TS, STT = dve.tensor_tensor, dve.tensor_scalar, dve.scalar_tensor_tensor

            def lo(u, k):
                dve.wait_ge(hi_done, u.at(k + 1))
                TT(w_lo[:, u.slot(k)], stage[:, u.slot(k)], w_hi[:, u.slot(k)].bitcast(F32), ALU.subtract).then_inc(lo_done, 1)

            def times_c(a, k, kt, to=acc, first=False):
                dve.wait_ge(ada_full[a.slot(k)], a.landed(k))
                if a.base + k:
                    dve.wait_ge(ada_done, a.at(k))
                cc = cact[:, kt:kt + 1] if isinstance(kt, int) else cact[:, ds(kt, 1)]
                if first:
                    TS(to[:], ada[:, a.slot(k)], cc, None, ALU.mult).then_inc(ada_done, 1)
                else:
                    STT(out=to[:], in0=ada[:, a.slot(k)], scalar=cc, in1=to[:], op0=ALU.mult, op1=ALU.add).then_inc(ada_done, 1)

            def clear_acc():
                own(dve.memset(acc[:], 0.0))

            def take_mod(chunk):
                dve.wait_ge(mod_red, chunk + 1)
                m = slice(MOD_TILE[chunk], MOD_TILE[chunk] + ADA_COLS)
                TT(mod[:, m], modp, V_BADA[:, m], ALU.add).then_inc(mod_ready, 1)

            def lo_of(xn, shift, x_hi, x_lo, pair, hi_there, ready):
                dve.wait_ge(hi_there, pair + 1)
                for j in range(2):
                    kt = 2 * pair + j
                    f = STT(out=x_lo[:, kt], in0=xn(kt), scalar=shift(kt), in1=x_hi[:, kt].bitcast(F32), op0=ALU.add, op1=ALU.subtract)
                f.then_inc(ready, 1)

            dve.wait_ge(vec_tr, 5)
            own(dve.tensor_copy(vec[:, 0], b56[:, 0, 0:P]))
            dve.tensor_copy(vec[:, 1, 0:118], b56[:, 0, P:P + 118]).then_inc(vec_ready, 1)
            own(dve.tensor_copy(vec[:, 2, 0:88], b56[:, 1, 0:88]))
            own(dve.tensor_copy(vec[:, 3, 0:88], b56[:, 1, P:P + 88]))
            dve.tensor_copy(vec[:, 4, 0:88], b56[:, 2, 0:88]).then_inc(vec_ready, 1)
            dve.wait_ge(x_tr, 16)
            dve.tensor_copy(xT[:, 8:10], b4[:].rearrange("p (a t) -> p a t", a=2)).then_inc(xT_dve, 1)
            dve.tensor_copy(xT[:, 10:14], b56[:]).then_inc(xT_dve, 1)
            dve.tensor_copy(xT[:, 14:16], b7[:].rearrange("p (a t) -> p a t", a=2)).then_inc(xT_dve, 1)
            dve.wait_ge(cact_ready, 1)
            a = Run(0)
            u = Run(0)

            def gain1(half):
                tiles = slice(8 * half, 8 * half + 8)
                own(STT(out=a1[:, tiles], in0=mod[:, KT + 8 * half:KT + 8 * half + 8], scalar=1.0, in1=V_G1[:, tiles], op0=ALU.add, op1=ALU.mult))

            def xn_of(pair):
                for kt in (2 * pair, 2 * pair + 1):
                    f = STT(out=xn[:, kt], in0=xT[:, kt], scalar=a1[:, kt:kt + 1], in1=rstd[:, 0], op0=ALU.mult, op1=ALU.mult)
                f.then_inc(hf_done, 1)

            def h_lo_of(pair):
                lo_of(lambda kt: xn[:, kt], lambda kt: mod[:, kt:kt + 1], h_hi, h_lo, pair, hhi_done, h_ready)

            for n in range(4 * KT):
                times_c(a, n, n % KT, (acc, acc_odd)[n // KT % 2], n % KT == 0)
                if n == 10:
                    dve.wait_ge(snk_ps, 1)
                    dve.tensor_copy(snk[:], b4[:, 16:32]).then_inc(snk_ready, 1)
                if n == 19:
                    take_mod(0)
                if n == 28:
                    dve.wait_ge(wgl_hi_done, 1)
                    TT(wgl_lo[:], wgl[:], wgl_hi[:].bitcast(F32), ALU.subtract).then_inc(wgl_ready, 1)
                if n == 33:
                    take_mod(1)
                    dve.wait_ge(mod_ready, 2)
                    dve.wait_ge(n1_rstd, 1)
                    dve.wait_ge(xsq_done, 4)
                    gain1(0)
                    xn_of(0)
                if 34 <= n < 38:
                    if n < 37:
                        xn_of(n - 33)
                    h_lo_of(n - 34)
                if n == 61:
                    take_mod(2)
            take_mod(3)
            dve.wait_ge(mod_ready, 4)
            gain1(1)
            for pair in range(4, 9):
                if pair < 8:
                    xn_of(pair)
                if pair > 4:
                    h_lo_of(pair - 1)
            clear_acc()
            dve.wait_ge(lo_done, 16)

            for b, (first, end, done) in enumerate(QK_STEPS):
                for k in range(first, end):
                    lo(u, k)
                dve.wait_ge(qk_rstd, b + 1)
                if b == 0:
                    STT(out=kT[:], in0=ps[:, 0, 0:2], scalar=V_KG, in1=rstd[:, 0:2], op0=ALU.mult, op1=ALU.mult).then_inc(k_ready, 1)
                    dve.tensor_copy(vt[:], ps[:, 0, 2:4]).then_inc(ps_free[0], 1)
                else:
                    dst = qT[:, 4 * (b - 1):4 * b]
                    STT(out=dst, in0=ps[:, 1] if b == 1 else b56[:], scalar=V_QG, in1=rstd[:], op0=ALU.mult, op1=ALU.mult).then_inc(ps_free[b % 2], 1)
            dve.wait_ge(glr_ps, 1)
            dve.tensor_copy(glr[:], b4[:, T:T + 2 * LR].rearrange("p (a n) -> p a n", a=2)).then_inc(glr_sb, 1)

            dve.wait_ge(rel_out, 16)
            with dve.Fori(0, 2) as i:
                for b in range(2):
                    u = Run(U_GQK + 8 * b, i, 16)
                    a = Run(KT * 4 + 4 * b, i, 8)
                    for k in range(AHEAD, 8 + AHEAD):
                        lo(u, k)
                        if k < 8:
                            times_c(a, k - 4, i * 8 + (4 * b + k - 4))
                    dve.wait_ge(used, u.at(8))
                    TS(gqk[:, ds(i * 8 + 4 * b, 4)], ps[:, (1 + b) % 2], 1.0, None, ALU.mult).then_inc(ps_free[(1 + b) % 2], 1)
            dve.wait_ge(glrT_ps, 2)
            dve.tensor_copy(glrT[:], b4[0:LR, T:2 * T]).then_inc(glrT_sb, 1)
            take_mod(4)

            def exponents(h):
                cum = lg[:, 2 * h:2 * h + 2].rearrange("p t (c j) -> p t c j", j=CH)
                last = cum[:, :, :, CH - 1:CH]
                q3 = qx[:].rearrange("p t (c j) -> p t c j", j=CH)
                own(TT(kx[:].rearrange("p t (c j) -> p t c j", j=CH), last[:, :, 0:3].broadcast_to([P, 2, 3, CH]),
                       cum[:, :, 0:3], ALU.subtract))
                own(TT(q3[:, :, 0:3:2], cum[:, :, 2:4], last[:, :, 1:3].broadcast_to([P, 2, 2, CH]), ALU.add))
                TT(q3[:, :, 1:2], q3[:, :, 2:3], last[:, :, 1:2].broadcast_to([P, 2, 1, CH]), ALU.add).then_inc(gla_arg, 1)

            def decayed(h):
                qv = gqk[:, 2 * h:2 * h + 2]
                kv = gqk[:, 8 + 2 * h:10 + 2 * h]
                dve.wait_ge(gla_exp, 4 * h + 4)
                own(STT(out=qd[:], in0=qv, scalar=DK ** -0.5, in1=eg[:], op0=ALU.mult, op1=ALU.mult))
                own(TT(ki[:], kv, en[:], ALU.mult))
                own(TT(kx[:], kv[:, :, 0:3 * CH], kx[:], ALU.mult))
                own(STT(out=qx[:, :, 0:2 * CH], in0=qv[:, :, 2 * CH:T], scalar=DK ** -0.5, in1=qx[:, :, 0:2 * CH], op0=ALU.mult, op1=ALU.mult))
                STT(out=qx[:, :, 2 * CH:3 * CH], in0=qv[:, :, 3 * CH:T], scalar=DK ** -0.5, in1=qx[:, :, 2 * CH:3 * CH], op0=ALU.mult, op1=ALU.mult).then_inc(gla_ready, 1)

            def attended_lo(g):
                dve.wait_ge(yahi_done, g + 1)
                TT(ya_lo[:, 2 * g:2 * g + 2].rearrange("p t (n q) -> p t n q", n=2),
                   b7[:].rearrange("p (n t q) -> p t n q", n=2, t=2),
                   ya_hi[:, 2 * g:2 * g + 2].rearrange("p t (n q) -> p t n q", n=2).bitcast(F32), ALU.subtract).then_inc(ya_ready, 1)

            for g in range(4):
                u = Run(U_GV + 8 * g)
                a = Run(KT * 5 + 4 * g)
                par = (1 + g) % 2
                lo(u, 4)
                times_c(a, 0, 4 * g, first=g == 0)
                lo(u, 5)
                times_c(a, 1, 4 * g + 1)
                dve.wait_ge(lnp_ready, g + 1)
                dve.wait_ge(keep_ready, 1)
                own(STT(out=lg[:, 2 * g:2 * g + 2], in0=lg[:, 2 * g:2 * g + 2], scalar=0.0, in1=lnp[:], op0=ALU.min, op1=ALU.subtract))
                own(dve.tensor_tensor_scan(lg[:, 2 * g], keep[:], lg[:, 2 * g], 0.0, ALU.mult, ALU.add))
                dve.tensor_tensor_scan(lg[:, 2 * g + 1], keep[:], lg[:, 2 * g + 1], 0.0, ALU.mult, ALU.add).then_inc(lg_ready, 1)
                lo(u, 6)
                if g:
                    attended_lo(g - 1)
                times_c(a, 2, 4 * g + 2)
                lo(u, 7)
                dve.wait_ge(scored, g + 1)
                dve.wait_ge(bias_ready, 2)
                if g:
                    dve.wait_ge(p_tr, g)
                for half in range(2):
                    heads = bias[:, 4 * g + half:4 * g + 4:2, :]
                    even0 = (b7[:, 0:T] if half == 0 else hi_b4).rearrange("p (h k) -> p h k", h=2)
                    own.note(STT(out=p0[:, half:NT:2], in0=even0, scalar=DH ** -0.5, in1=heads[:, :, P:2 * P], op0=ALU.mult, op1=ALU.add))
                    f = STT(out=p1[:, half:NT:2], in0=b56[:, 2 * half:2 * half + 2], scalar=DH ** -0.5, in1=heads, op0=ALU.mult, op1=ALU.add)
                    own.note(f) if half == 0 else own(f)
                own.note(dve.tensor_reduce(mx[:, 0], p0[:], AX.X, ALU.max))
                own(dve.tensor_reduce(mx[:, 1], p1[:], AX.X, ALU.max))
                sink = snk[:, 4 * g:4 * g + 4].unsqueeze(1).broadcast_to([P, 2, NT])
                own(TT(mx[:], mx[:], sink, ALU.max))
                own(TS(nmx[:], mx[:], -1.0, None, ALU.mult))
                TT(esk[:], sink, mx[:], ALU.subtract).then_inc(m_ready, 1)
                lo(u, 8)
                times_c(a, 3, 4 * g + 3)
                if g < 3:
                    lo(u, 9)
                dve.wait_ge(exped, g + 1)
                own(TT(rsum[:], rsum[:], esk[:], ALU.add))
                own(dve.reciprocal(rsum[:], rsum[:]))
                own(TT(p0[:], p0[:], rsum[:, 0].unsqueeze(2).broadcast_to([P, NT, P]), ALU.mult))
                TT(p1[:], p1[:], rsum[:, 1].unsqueeze(2).broadcast_to([P, NT, 2 * P]), ALU.mult).then_inc(p_ready, 1)
                for k in range(10 if g < 3 else 9, 12):
                    lo(u, k)
                dve.wait_ge(used, u.at(8))
                dve.wait_ge(xs_out, 16)
                dve.tensor_copy(gv[:, g], ps_tok[:, par]).then_inc(ps_free[par], 1)
            dve.wait_ge(lg_ready, 4)
            exponents(0)
            take_mod(5)
            attended_lo(3)
            decayed(0)

            for n in range(GH):
                par = (1 + n) % 2
                u = Run(U_GR + 8 * n)
                a = Run(KT * 6 + 4 * n)
                lo(u, 4)
                times_c(a, 0, 4 * n, first=n == 0)
                lo(u, 5)
                times_c(a, 1, 4 * n + 1)
                if n < GH - 1:
                    dve.wait_ge(at_ps, n + 1)
                    exponents(n + 1)
                lo(u, 6)
                times_c(a, 2, 4 * n + 2)
                lo(u, 7)
                if n < GH - 1:
                    decayed(n + 1)
                lo(u, 8)
                times_c(a, 3, 4 * n + 3)
                lo(u, 9)
                lo(u, 10)
                dve.wait_ge(rsg_ready, n + 1)
                for j in range(NT):
                    f = STT(out=yt[:, j], in0=b56[:, j], scalar=V_GG[:, j:j + 1], in1=rsg[:], op0=ALU.mult, op1=ALU.mult)
                    own.note(f) if j < NT - 1 else own(f)
                lo(u, 11)
                dve.wait_ge(ps_free[par], 6 + n // 2 + n % 2)
                TT(yt[:], yt[:], sil[:], ALU.mult).then_inc(yt_ready, 1)
                dve.wait_ge(yghi_done, n + 1)
                TT(yg_lo[:, 4 * n:4 * n + 4], yt[:], yg_hi[:, 4 * n:4 * n + 4].bitcast(F32), ALU.subtract).then_inc(yg_ready, 1)
            take_mod(6)
            clear_acc()
            own(dve.memset(sqsum[:], 0.0))

            with dve.Fori(0, 4) as i:
                own.enter(i, 1)
                a = Run(KT * 7, i, KT)
                kt = 0
                first = 0
                for b, (units, extra) in enumerate(((8, (1, 1, 1, 2)), (8, (1, 1, 1, 2)), (4, ()), (8, (1, 2, 1, 2)))):
                    u = Run(U_MERGE + first, i, MERGE_UNITS)
                    par = (1 + b) % 2
                    for k in range(AHEAD, units + AHEAD):
                        lo(u, k)
                        for _ in range(extra[k - 4] if k < 8 and extra else 0):
                            times_c(a, kt, kt)
                            kt += 1
                    if b >= 2:
                        dve.wait_ge(used, u.at(units))
                        dve.wait_ge(ps_free[par], i * 2 + (6 + b))
                        if b == 2:
                            TT(mrg[:], ps[:, par], sig_a[:], ALU.mult).then_inc(ps_free[par], 1)
                        else:
                            TT(mrg2[:], ps[:, par], sig_b[:], ALU.mult).then_inc(ps_free[par], 1)
                            dve.wait_ge(ps_free[1], i * 2 + 9)
                            dve.wait_ge(ps_free[0], i * 2 + 10)
                            TT(mrg[:], mrg[:], mrg2[:], ALU.add).then_inc(mrg_ready, 1)
                            dve.wait_ge(mhi_done, i + 1)
                            TT(m_lo[:, ds(i * 4, 4)], mrg[:], m_hi[:, ds(i * 4, 4)].bitcast(F32), ALU.subtract).then_inc(m_done, 1)
                    first += units
                dve.wait_ge(mod_red, i + 8)
                TT(mod[:, ds(i * 8 + 56, 8)], modp, vec[:, 0, ds(i * 8 + 56, 8)], ALU.add).then_inc(mod_ready, 1)
                clear_acc()
                own.leave(4)

            with dve.Fori(0, 2) as i:
                own.enter(i, 2 * 1)
                for b in range(2):
                    par = (1 + b) % 2
                    u = Run(U_WOUT + 8 * b, i, 16)
                    a = Run(KT * 11 + 4 * b, i, 8)
                    for k in range(AHEAD, 7 + AHEAD):
                        lo(u, k)
                        if k < 8:
                            times_c(a, k - 4, i * 8 + (4 * b + k - 4))
                    dve.wait_ge(x_back, 16)
                    dve.wait_ge(mod_ready, 11)
                    dve.wait_ge(out_half, i * 2 + (b + 1))
                    for j in range(NT):
                        if j == 2:
                            dve.wait_ge(used, u.at(8))
                        xt = x1[:, ds(i * 8 + (4 * b + j), 1)]
                        f = STT(out=xt, in0=ps[:, par, j:j + 1], scalar=mod[:, ds(i * 8 + (32 + 4 * b + j), 1)], in1=xt, op0=ALU.mult, op1=ALU.add)
                        if j % 2:
                            f.then_inc(x1_done, 1)
                    dve.wait_ge(x1sq_done, i * 4 + (2 * b + 1))
                    own(TT(sqsum[:], sqsum[:], xsq2[:, 0:2], ALU.add))
                    dve.wait_ge(x1sq_done, i * 4 + (2 * b + 2))
                    TT(sqsum[:], sqsum[:], xsq2[:, 2:4], ALU.add).then_inc(ps_free[par], 1)
                    dve.wait_ge(ps_free[par], i + (16 + b))
                    lo(u, 7 + AHEAD)
                own.leave(2)
            take_mod(11)
            dve.wait_ge(mod_ready, 12)
            own(STT(out=a2[:], in0=mod[:, 4 * KT:5 * KT], scalar=1.0, in1=V_G2, op0=ALU.add, op1=ALU.mult))
            dve.wait_ge(n2_rstd, 1)

            def h2_lo_of(pair):
                lo_of(lambda kt: xr[:, kt % 4], lambda kt: mod[:, 3 * KT + kt:3 * KT + kt + 1], h2_hi, h2_lo, pair, h2hi_done, h2_ready)

            for pair in range(8):
                if pair >= 2:
                    dve.wait_ge(h2_ready, pair - 1)
                for kt in (2 * pair, 2 * pair + 1):
                    f = STT(out=xr[:, kt % 4], in0=x1[:, kt], scalar=a2[:, kt:kt + 1], in1=rs2[:], op0=ALU.mult, op1=ALU.mult)
                f.then_inc(h2f, 1)
                if pair:
                    h2_lo_of(pair - 1)
            h2_lo_of(7)

            for k in range(AHEAD, 8 + AHEAD):
                lo(Run(U_UP), k)
            with dve.Fori(0, UP_STEPS) as i:
                own.enter(i, 2 * 7)
                for b, cv in enumerate((cva, cvb)):
                    par = (1 + b) % 2
                    u = Run(U_UP + 8 * b, i, 16)
                    for k in range(8):
                        lo(u, 8 + AHEAD + k)
                        if k < 2:
                            tiles = (2 * k, 2 * k + 1)
                            dve.wait_ge(cv0, i * 8 + (4 * b + 2 * k + 2))
                            for j in tiles:
                                f = STT(out=cv[:, j, 1:T], in0=ps[:, par, j, 0:T - 1], scalar=vec[:, 3, ds(i * NT + (b * FT + j), 1)],
                                        in1=cv[:, j, 1:T], op0=ALU.mult, op1=ALU.add)
                                own.note(f) if j % 2 == 0 else own(f)
                            for j in tiles:
                                f = STT(out=cv[:, j, 2:T], in0=ps[:, par, j, 0:T - 2], scalar=vec[:, 2, ds(i * NT + (b * FT + j), 1)],
                                        in1=cv[:, j, 2:T], op0=ALU.mult, op1=ALU.add)
                                f.then_inc(ps_free[par], 1) if j == NT - 1 else own.note(f)
                        if k == 3 and b == 1:
                            dve.wait_ge(ps_free[0], i + 19)
                            dve.wait_ge(sil_done, i + 1)
                            TT(cvb[:], cva[:], cvb[:], ALU.mult).then_inc(gf_done, 1)
                        if k == 5 and b == 1:
                            dve.wait_ge(ghi_done, i + 1)
                            TT(g_lo[:, ds(i * NT, NT)], cvb[:], g_hi[:, ds(i * NT, NT)].bitcast(F32), ALU.subtract).then_inc(g_ready, 1)
                own.leave(UP_STEPS)

            for b in range(4):
                par = (1 + b) % 2
                u = Run(U_DOWN + b * DOWN_UNITS)
                for k in range(8 + AHEAD if b == 0 else AHEAD, DOWN_UNITS - 1 + AHEAD):
                    if u.base + k < UNITS:
                        lo(u, k)
                dve.wait_ge(down_half, b + 1)
                if b >= 2:
                    dve.wait_ge(y_tr, b - 1)
                if b == 0:
                    dve.wait_ge(g_ready, UP_STEPS)
                for j in range(NT):
                    kt = 4 * b + j
                    if j == 2:
                        dve.wait_ge(used, u.at(DOWN_UNITS))
                    STT(out=ytmp[:, par, j], in0=ps[:, par, j], scalar=mod[:, 5 * KT + kt:5 * KT + kt + 1], in1=x1[:, kt], op0=ALU.mult, op1=ALU.add).then_inc(y_tile, 1)
                if b < 3:
                    lo(u, DOWN_UNITS - 1 + AHEAD)

        @block.tensor
        def _(pe):
            def mm(out, lhsT, rhs, start, stop=False):
                return pe.matmul(out, lhsT, rhs, start=start, stop=stop, skip_group_check=True)

            def last_unit(u, k, par, xh, xl, half_done):
                pe.wait_ge(lo_done, u.at(k + 1))
                s = u.slot(k)
                for j in range(NT):
                    cols = slice(j * P, (j + 1) * P)
                    for q in range(2):
                        kt = 2 * k + q
                        mm(ps[:, par, j], w_hi[:, s, q, cols], xh[:, kt], False)
                        mm(ps[:, par, j], w_hi[:, s, q, cols], xl[:, kt], False)
                        f = mm(ps[:, par, j], w_lo[:, s, q, cols], xh[:, kt], False, q == 1)
                    if j == 1:
                        f.then_inc(half_done, 1)
                f.then_inc(used, 1)

            def unit(u, k, par, xh, xl, last, kind="feature"):
                pe.wait_ge(lo_done, u.at(k + 1))
                s = u.slot(k)
                for q in range(2):
                    kt = 2 * k + q
                    end = last and q == 1
                    if kind in ("feature", "keys+values"):
                        for j in range(NT if kind == "feature" else 2):
                            cols = slice(j * P, (j + 1) * P)
                            o = ps[:, par, j] if par < 2 else b56[:, j]
                            mm(o, w_hi[:, s, q, cols], xh[:, kt], kt == 0 and j % 2 == 0)
                            mm(o, w_hi[:, s, q, cols], xl[:, kt], False)
                            f = mm(o, w_lo[:, s, q, cols], xh[:, kt], False, end)
                    if kind == "keys+values":
                        for t in range(2):
                            o = ps[:, par, 2 + t]
                            tok = slice(t * P, (t + 1) * P)
                            mm(o, xh[:, kt, tok], w_hi[:, s, q, T:2 * T], kt == 0 and t == 0)
                            mm(o, xl[:, kt, tok], w_hi[:, s, q, T:2 * T], False)
                            f = mm(o, xh[:, kt, tok], w_lo[:, s, q, T:2 * T], False, end)
                    if kind == "token":
                        for t in range(2):
                            o = ps_tok[:, par, t]
                            tok = slice(t * P, (t + 1) * P)
                            mm(o, xh[:, kt, tok], w_hi[:, s, q], kt == 0)
                            mm(o, xl[:, kt, tok], w_hi[:, s, q], False)
                            f = mm(o, xh[:, kt, tok], w_lo[:, s, q], False, end)
                f.then_inc(used, 1)

            def free(par, n):
                pe.wait_ge(ps_free[par], n)

            def reduce_mod(chunk):
                pe.wait_ge(ada_done, (chunk + 1) * KT)
                if chunk:
                    pe.wait_ge(mod_ready, chunk)
                sums = acc_odd if chunk in (1, 3) else acc
                for j in range(ADA_COLS):
                    f = mm(b4[:, j:j + 1], sums[:, j * P:(j + 1) * P], ones[:, 0:1], True, True)
                f.then_inc(mod_red, 1)

            pe.wait_ge(consts, 1)
            pe.wait_ge(vec_in, 16 * 14)
            for n, r in enumerate((P, 118, 88, 88, 88)):
                dst = b56[:, n // 2, (n % 2) * P:(n % 2) * P + r]
                pe.transpose(dst, vrows[0:r, n, :], ident[0:r, 0:r]).then_inc(vec_tr, 1)
            pe.wait_ge(x_in, 16)
            for kt in range(KT):
                if kt < 8:
                    dst = ps[:, kt // 4, kt % 4]
                elif kt < 10:
                    dst = b4[:, (kt - 8) * T:(kt - 7) * T]
                elif kt < 14:
                    dst = b56[:, kt - 10]
                else:
                    dst = b7[:, (kt - 14) * T:(kt - 13) * T]
                if kt == 8:
                    pe.wait_ge(vec_ready, 2)
                for t in range(2):
                    f = pe.transpose(dst[:, t * P:(t + 1) * P], x_tok[:, t, kt * P:(kt + 1) * P], ident[:])
                f.then_inc(x_tr, 1)
            pe.wait_ge(misc_in, 16 * 5)
            pe.wait_ge(xT_dve, 3)
            mm(b4[:, 16:32], ones[0:1, :], snkrow[:], True, True).then_inc(snk_ps, 1)
            for kt in range(KT):
                if kt % 4 == 0:
                    pe.wait_ge(xsq_done, kt // 4 + 1)
                f = mm(b7[:, 0:T], ones[:], x_sq[:, kt], kt == 0, kt == KT - 1)
            f.then_inc(n1_sum, 1)
            pe.wait_ge(vec_ready, 2)
            mm(b56[0:HQ, 0, 0:P], relt[:], hot[:], True, True).then_inc(rel_ps, 1)
            pe.wait_ge(snk_ready, 1)
            reduce_mod(0)
            reduce_mod(1)

            def head_sums(b):
                pe.wait_ge(qk_sq, b + 1)
                if b:
                    free(0, 1)
                if b == 2:
                    pe.wait_ge(qk_rstd, 2)
                for j in range(0, NT if b else 2, 2):
                    dst = ps[:, 0, j:j + 2] if b else b7[:].rearrange("p (j t) -> p j t", j=2)
                    f = mm(dst, halves[:], sq[:, j:j + 2], True, True)
                f.then_inc(qk_sum, 1)

            pe.wait_ge(xT_act, 2)
            pe.wait_ge(n1_rstd, 1)
            for half in range(2):
                for b in range(3):
                    if b == 2:
                        pe.wait_ge(rel_sb, 1)
                    for k in range(4 * half, 4 * half + 4):
                        if b == 0:
                            pe.wait_ge(h_ready, k + 1)
                        unit(Run(8 * half + 4 * b), k, b, h_hi, h_lo, k == 7, "feature" if b else "keys+values")
                        if b and k == 4:
                            head_sums(b - 1)
                if half == 0:
                    reduce_mod(2)
                    reduce_mod(3)
            pe.wait_ge(wgl_ready, 1)
            pe.wait_ge(mod_ready, 4)
            for t in range(2):
                tok = slice(t * P, (t + 1) * P)
                o = b4[:, T + t * LR:T + (t + 1) * LR]
                for kt in range(KT):
                    mm(o, h_hi[:, kt, tok], wgl_hi[:, kt], kt == 0)
                    mm(o, h_lo[:, kt, tok], wgl_hi[:, kt], False)
                    f = mm(o, h_hi[:, kt, tok], wgl_lo[:, kt], False, kt == KT - 1)
            f.then_inc(glr_ps, 1)
            head_sums(2)

            with pe.Fori(0, 2) as i:
                for b in range(2):
                    u = Run(U_GQK + 8 * b, i, 16)
                    free((1 + b) % 2, i + (1 + b))
                    for k in range(8):
                        unit(u, k, (1 + b) % 2, h_hi, h_lo, k == 7)

            pe.wait_ge(glr_sb, 1)
            for t in range(2):
                pe.transpose(b4[0:LR, T + t * P:T + (t + 1) * P], glr[:, t], ident[:]).then_inc(glrT_ps, 1)

            def scores(g):
                for t in range(NT):
                    half = t % 2
                    rows = slice(DH * half, DH * (half + 1))
                    q = qT[rows, 2 * g + t // 2]
                    kk = (kT if g % 2 == half else kS)[rows, g // 2]
                    mm(b56[:, 2 * half + t // 2], q[:, P:2 * P], kk, True, True)
                    o = b7[:, (t // 2) * P:(t // 2 + 1) * P] if half == 0 else b4[:, T + (t // 2) * P:T + (t // 2 + 1) * P]
                    f = mm(o, q[:, 0:P], kk[:, 0:P], True, True)
                f.then_inc(scored, 1)

            def probs_back(g):
                pe.wait_ge(p_ready, g + 1)
                for t in range(NT):
                    pe.transpose(b7[:, t * P:(t + 1) * P], p0[:, t], ident[:])
                for kb in range(2):
                    for t in range(NT):
                        f = pe.transpose(b56[:, 2 * kb + t // 2, (t % 2) * P:(t % 2 + 1) * P], p1[:, t, kb * P:(kb + 1) * P], ident[:])
                f.then_inc(p_tr, 1)

            def attend(g):
                pe.wait_ge(pt_ready, g + 1)
                for half in range(2):
                    rows = slice(DH * half, DH * (half + 1))
                    vals = [vt[:, kb, g * DH:(g + 1) * DH] for kb in range(2)]
                    probs = [pt[:, n].rearrange("p (h q) -> p h q", q=P)[:, half:NT:2] for n in range(3)]
                    mm(b7[rows, 0:T], vals[0], probs[0], True, True)
                    mm(b7[rows, T:2 * T], vals[0], probs[1], True)
                    f = mm(b7[rows, T:2 * T], vals[1], probs[2], False, True)
                f.then_inc(pv_done, 1)

            pe.wait_ge(k_swapped, 32)
            for g in range(4):
                par = (1 + g) % 2
                u = Run(U_GV + 8 * g)
                free(par, (7 + g) // 2)
                for k in range(8):
                    unit(u, k, par, h_hi, h_lo, k == 7, "token")
                    if g == 0 and k == 0:
                        pe.wait_ge(glrT_sb, 1)
                        reduce_mod(4)
                        pe.wait_ge(qk_rstd, 3)
                        for m in range(8):
                            if m == 6:
                                pe.wait_ge(z_sb, 4)
                            zp = b56[:, m] if m < 4 else b7[:, (m - 4) * T:(m - 3) * T] if m < 6 else b56[:, m - 6]
                            mm(zp, wgk_s[:, m * P:(m + 1) * P], glrT[:], True, True).then_inc(z_ps, 1)
                    if g and k == 1:
                        probs_back(g - 1)
                    if g and k == 2:
                        attend(g - 1)
                    if k == 4:
                        if g:
                            pe.wait_ge(ya_ready, g)
                        else:
                            pe.wait_ge(z_sb, 8)
                            pe.wait_ge(mod_ready, 5)
                        scores(g)
            probs_back(3)
            reduce_mod(5)
            attend(3)

            with pe.Fori(0, 2) as i:
                for b in range(2):
                    n = i * 2 + b
                    par = (1 + b) % 2
                    u = Run(U_GR + 8 * b, i, 16)
                    free(par, i + (5 + b))
                    for k in range(2):
                        unit(u, k, par, h_hi, h_lo, False)
                    pe.wait_ge(ya_ready, 4)
                    pe.wait_ge(gla_ready, n + 1)
                    lo64, hi64 = slice(0, CH), slice(CH, P)
                    for rows, c0, w, keys, k0, queries, q0 in (
                            (lo64, 0, CH, ki, 0, qd, 0), (lo64, CH, CH, kx, 0, qd, CH), (lo64, 2 * CH, 2 * CH, kx, 0, qx, 0),
                            (lo64, T, CH, ki, 2 * CH, qd, 2 * CH), (lo64, T + CH, CH, kx, 2 * CH, qd, 3 * CH),
                            (hi64, CH, CH, ki, CH, qd, CH), (hi64, 2 * CH, CH, kx, CH, qd, 2 * CH), (hi64, 3 * CH, CH, kx, CH, qx, 2 * CH),
                            (hi64, T + CH, CH, ki, 3 * CH, qd, 3 * CH)):
                        for q in range(2):
                            f = mm(b7[rows, c0:c0 + w], keys[:, q, k0:k0 + CH], queries[:, q, q0:q0 + w], q == 0, q == 1)
                    f.then_inc(at_ps, 1)
                    for k in range(2, 5):
                        unit(u, k, par, h_hi, h_lo, False)
                    pe.wait_ge(at_ready, i * 4 + (2 * b + 2))
                    pe.wait_ge(gvh_ready, n + 1)
                    for j in range(NT):
                        cols = slice(j * P, (j + 1) * P)
                        mm(b56[:, j], gvh[:, 0, cols], at[:, 0:T], j % 2 == 0)
                        f = mm(b56[:, j, P:T], gvh[:, 1, cols], at[:, T:T + P], False, True)
                    f.then_inc(o_ps, 1)
                    for k in range(5, 7):
                        unit(u, k, par, h_hi, h_lo, False)
                    pe.wait_ge(osq_sum, n + 1)
                    pe.wait_ge(mod_ready, 6)
                    mm(hi_b4, ones[:], osq[:, 0], True, True).then_inc(oss_ps, 1)
                    unit(u, 7, par, h_hi, h_lo, True)
            pe.wait_ge(rsg_ready, 4)
            reduce_mod(6)

            with pe.Fori(0, 4) as i:
                first = 0
                for b, (units, xh, xl) in enumerate(((8, h_hi, h_lo), (8, h_hi, h_lo), (4, ya_hi, ya_lo), (8, yg_hi, yg_lo))):
                    par = (1 + b) % 2
                    u = Run(U_MERGE + first, i, MERGE_UNITS)
                    free(par, i * 2 + (7 + (b + 1) // 2))
                    if b == 3:
                        pe.wait_ge(yg_ready, 4)
                    for k in range(units):
                        unit(u, k, par, xh, xl, k == units - 1)
                    first += units
                pe.wait_ge(ada_done, i * KT + 8 * KT)
                pe.wait_ge(mod_ready, i + 7)
                for j in range(ADA_COLS):
                    f = mm(b4[:, j:j + 1], acc[:, j * P:(j + 1) * P], ones[:, 0:1], True, True)
                f.then_inc(mod_red, 1)

            with pe.Fori(0, 2) as i:
                for b in range(2):
                    par = (1 + b) % 2
                    u = Run(U_WOUT + 8 * b, i, 16)
                    free(par, i + (15 + b))
                    for k in range(8):
                        if k >= 6:
                            pe.wait_ge(m_done, 4)
                        elif k % 2 == 0:
                            pe.wait_ge(m_done, k // 2 + 1)
                        if k < 7:
                            unit(u, k, par, m_hi, m_lo, False)
                        else:
                            last_unit(u, k, par, m_hi, m_lo, out_half)
            reduce_mod(11)
            pe.wait_ge(ps_free[0], 18)
            mm(b7[:, 0:T], ones[:], sqsum[:, 0], True)
            mm(b7[:, 0:T], ones[:], sqsum[:, 1], False, True).then_inc(n2_sum, 1)

            with pe.Fori(0, UP_STEPS) as i:
                for b in range(2):
                    par = (1 + b) % 2
                    u = Run(U_UP + 8 * b, i, 16)
                    free(par, i + (17 + b))
                    for k in range(8):
                        if b == 0:
                            pe.wait_ge(h2_ready, k + 1)
                        unit(u, k, par, h2_hi, h2_lo, k == 7)

            with pe.Fori(0, 2) as i:
                def back(b):
                    for j in range(NT):
                        pe.wait_ge(y_tile, i * 8 + (4 * b + j + 1))
                        for t in range(2):
                            f = pe.transpose(b56[:, 2 * t + j // 2, (j % 2) * P:(j % 2 + 1) * P],
                                             ytmp[:, (1 + b) % 2, j, t * P:(t + 1) * P], ident[:])
                    f.then_inc(y_tr, 1)

                for b in range(2):
                    par = (1 + b) % 2
                    u = Run(U_DOWN + DOWN_UNITS * b, i, 2 * DOWN_UNITS)
                    pe.wait_ge(ps_free[par], 28 + b)
                    for k in range(DOWN_UNITS):
                        if b == 0 and k % 2 == 0:
                            pe.wait_ge(g_ready, k // 2 + 1)
                        if k < DOWN_UNITS - 1:
                            unit(u, k, par, g_hi, g_lo, False)
                        else:
                            last_unit(u, k, par, g_hi, g_lo, down_half)
                        if b == 1 and k == 1:
                            back(0)
                back(1)


_INS = ["x", "c", "rel_bias_table", "w_ada", "b_ada", "norm1_gain", "w_in", "q_norm_gain", "k_norm_gain",
        "attn_sinks", "w_gk_up", "b_gk", "gla_norm_gain", "w_branch_attn", "w_branch_gla", "w_out",
        "norm2_gain", "w_ffn_up", "ffn_conv_w", "ffn_conv_b", "w_ffn_down"]


def kernel(**inputs):
    import concourse.bacc as bacc
    from concourse.bass_utils import run_bass_kernel_spmd

    nc = bacc.Bacc("TRN2", target_bir_lowering=False, num_devices=1)
    arrays = {f"in_{name}": np.ascontiguousarray(inputs[name]) for name in _INS}
    arrays["in_onehot"] = one_hot_distances()
    args = [nc.dram_tensor(n, a.shape, mybir.dt.from_np(a.dtype), kind="ExternalInput").ap() for n, a in arrays.items()]
    out = nc.dram_tensor("out", (1, T, D), F32, kind="ExternalOutput").ap()
    layer(nc, *args, out)
    r = run_bass_kernel_spmd(nc, [arrays], core_ids=[0])
    return r.results[0]["out"]
```
